# Optimizing a Trainium2 kernel written in Bass

```python
import jax
import jax.numpy as jnp
from jax import lax
import numpy as np

D_MODEL = 2048
BATCH = 1
SEQ = 256
DEPTH = 1

GRID_W = 64
CTX_LEN = 256
HEAD_DIM = 128
N_Q_HEADS = 16
N_KV_HEADS = 4
Q_PER_KV = N_Q_HEADS // N_KV_HEADS
ATTN_WIDTH = N_Q_HEADS * HEAD_DIM
KV_WIDTH = N_KV_HEADS * HEAD_DIM
N_FOURIER_GROUPS = 4
FOURIER_GROUP_DIM = 256
FOURIER_WIDTH = N_FOURIER_GROUPS * FOURIER_GROUP_DIM
N_BRANCHES = 2
Q_END = ATTN_WIDTH
K_END = Q_END + KV_WIDTH
V_END = K_END + KV_WIDTH
F_END = V_END + FOURIER_WIDTH
IN_WIDTH = F_END + N_BRANCHES * D_MODEL
D_FF = 4 * D_MODEL
N_MOD = 6
Q_BLOCK = 128
ROPE_THETA = 10000.0
ROPE_AXIS_PAIRS = HEAD_DIM // 4
EPS = 1e-6

kernel_name = 'hybrid_gqa_fnet_adaln_prefix_block'

def rmsnorm(x, g):
    xf = x.astype(jnp.float32)
    xf = xf * lax.rsqrt(jnp.mean(xf * xf, axis=-1, keepdims=True) + EPS)
    return (xf * g.astype(jnp.float32)).astype(x.dtype)

def modulate(h, shift, scale):
    return h * (1 + scale) + shift

def axial_rope_tables(rows):
    inv = 1.0 / (ROPE_THETA ** (jnp.arange(ROPE_AXIS_PAIRS, dtype=jnp.float32) / ROPE_AXIS_PAIRS))
    row_ang = jnp.arange(rows, dtype=jnp.float32)[:, None] * inv
    col_ang = jnp.arange(GRID_W, dtype=jnp.float32)[:, None] * inv
    ang = jnp.concatenate([
        jnp.broadcast_to(row_ang[:, None, :], (rows, GRID_W, ROPE_AXIS_PAIRS)),
        jnp.broadcast_to(col_ang[None, :, :], (rows, GRID_W, ROPE_AXIS_PAIRS))], axis=-1)
    ang = ang.reshape(rows * GRID_W, 2 * ROPE_AXIS_PAIRS)
    return jnp.cos(ang), jnp.sin(ang)

def apply_rope(x, cos, sin):
    xf = x.astype(jnp.float32).reshape(x.shape[:-1] + (HEAD_DIM // 2, 2))
    x1, x2 = xf[..., 0], xf[..., 1]
    c = cos[None, :, None, :]
    s = sin[None, :, None, :]
    out = jnp.stack([x1 * c - x2 * s, x1 * s + x2 * c], axis=-1)
    return out.reshape(x.shape).astype(x.dtype)

def heads(t, n_heads):
    return t.reshape(t.shape[0], t.shape[1], n_heads, HEAD_DIM)

def block_attention(q, k, v):
    b, n = q.shape[0], q.shape[1]
    nblk = n // Q_BLOCK
    qb = q.reshape(b, nblk, Q_BLOCK, N_KV_HEADS, Q_PER_KV, HEAD_DIM).transpose(1, 0, 2, 3, 4, 5)
    scale = HEAD_DIM ** -0.5

    def one_block(q_blk):
        s = jnp.einsum('bqhgd,bkhd->bhgqk', q_blk, k).astype(jnp.float32) * scale
        p = jax.nn.softmax(s, axis=-1).astype(v.dtype)
        return jnp.einsum('bhgqk,bkhd->bqhgd', p, v)

    o = lax.map(one_block, qb)
    return o.transpose(1, 0, 2, 3, 4, 5).reshape(b, n, ATTN_WIDTH)

def fourier_mix(u):
    b, n = u.shape[0], u.shape[1]
    ug = u.astype(jnp.float32).reshape(b, n, N_FOURIER_GROUPS, FOURIER_GROUP_DIM)
    f = jnp.fft.fft2(ug, axes=(1, 3), norm='ortho').real
    return f.reshape(b, n, FOURIER_WIDTH).astype(u.dtype)

def merge_branches(attn_o, four_in, gate_logits, w_attn_o, w_fourier, w_out):
    a = attn_o @ w_attn_o
    f = fourier_mix(four_in) @ w_fourier
    g_a, g_f = jnp.split(gate_logits, N_BRANCHES, axis=-1)
    return (jax.nn.sigmoid(g_a) * a + jax.nn.sigmoid(g_f) * f) @ w_out

def sq_relu_mlp(h, w1, w2):
    return jnp.square(jax.nn.relu(h @ w1)) @ w2

def setup_inputs(seed: int = 0) -> dict:
    key = jax.random.key(seed)
    ks = jax.random.split(key, 17)

    def nrm(k, shape, scale):
        return jax.random.normal(k, shape, dtype=jnp.float32) * scale

    return {
        'x': nrm(ks[0], (BATCH, SEQ, D_MODEL), 1.0),
        'c': nrm(ks[1], (BATCH, D_MODEL), 1.0),
        'ctx': nrm(ks[2], (BATCH, CTX_LEN, D_MODEL), 1.0),
        'c_ctx': nrm(ks[3], (D_MODEL,), 1.0),
        'w_ada': nrm(ks[4], (DEPTH, D_MODEL, N_MOD * D_MODEL), 0.5 * D_MODEL ** -0.5),
        'b_ada': nrm(ks[5], (DEPTH, N_MOD * D_MODEL), 0.02),
        'norm1_g': 1.0 + nrm(ks[6], (DEPTH, D_MODEL), 0.02),
        'w_in': nrm(ks[7], (DEPTH, D_MODEL, IN_WIDTH), D_MODEL ** -0.5),
        'q_norm_g': 1.0 + nrm(ks[8], (DEPTH, HEAD_DIM), 0.02),
        'k_norm_g': 1.0 + nrm(ks[9], (DEPTH, HEAD_DIM), 0.02),
        'w_attn_o': nrm(ks[10], (DEPTH, ATTN_WIDTH, D_MODEL), ATTN_WIDTH ** -0.5),
        'w_fourier': nrm(ks[11], (DEPTH, FOURIER_WIDTH, D_MODEL), FOURIER_WIDTH ** -0.5),
        'w_out': nrm(ks[12], (DEPTH, D_MODEL, D_MODEL), D_MODEL ** -0.5),
        'norm2_g': 1.0 + nrm(ks[13], (DEPTH, D_MODEL), 0.02),
        'w1': nrm(ks[14], (DEPTH, D_MODEL, D_FF), D_MODEL ** -0.5),
        'w2': nrm(ks[15], (DEPTH, D_FF, D_MODEL), D_FF ** -0.5),
        'final_norm_g': 1.0 + nrm(ks[16], (D_MODEL,), 0.02),
    }

def reference(x, c, ctx, c_ctx, w_ada, b_ada, norm1_g, w_in, q_norm_g, k_norm_g,
              w_attn_o, w_fourier, w_out, norm2_g, w1, w2, final_norm_g):
    n_lat = x.shape[1]
    ROWS = n_lat // GRID_W
    cos, sin = axial_rope_tables(ROWS)
    xc = ctx
    for l in range(DEPTH):
        need_ctx_out = l < DEPTH - 1
        w_in_l = w_in[l]
        mod = jax.nn.silu(c) @ w_ada[l] + b_ada[l]
        mod_c = jax.nn.silu(c_ctx) @ w_ada[l] + b_ada[l]
        sh1, sc1, g1, sh2, sc2, g2 = jnp.split(mod[:, None, :], N_MOD, axis=-1)
        csh1, csc1, cg1, csh2, csc2, cg2 = jnp.split(mod_c, N_MOD, axis=-1)

        h = modulate(rmsnorm(x, norm1_g[l]), sh1, sc1)
        hc = modulate(rmsnorm(xc, norm1_g[l]), csh1, csc1)
        p = h @ w_in_l
        q = apply_rope(rmsnorm(heads(p[..., :Q_END], N_Q_HEADS), q_norm_g[l]), cos, sin)
        k = apply_rope(rmsnorm(heads(p[..., Q_END:K_END], N_KV_HEADS), k_norm_g[l]), cos, sin)
        v = heads(p[..., K_END:V_END], N_KV_HEADS)
        kc = rmsnorm(heads(hc @ w_in_l[:, Q_END:K_END], N_KV_HEADS), k_norm_g[l])
        vc = heads(hc @ w_in_l[:, K_END:V_END], N_KV_HEADS)
        k_all = jnp.concatenate([k, kc], axis=1)
        v_all = jnp.concatenate([v, vc], axis=1)
        o = block_attention(q, k_all, v_all)
        y = merge_branches(o, p[..., V_END:F_END], p[..., F_END:], w_attn_o[l], w_fourier[l], w_out[l])

        if need_ctx_out:
            qc = rmsnorm(heads(hc @ w_in_l[:, :Q_END], N_Q_HEADS), q_norm_g[l])
            pcr = hc @ w_in_l[:, V_END:]
            oc = block_attention(qc, kc, vc)
            yc = merge_branches(oc, pcr[..., :FOURIER_WIDTH], pcr[..., FOURIER_WIDTH:],
                                w_attn_o[l], w_fourier[l], w_out[l])
            xc = xc + cg1 * yc
            hc2 = modulate(rmsnorm(xc, norm2_g[l]), csh2, csc2)
            xc = xc + cg2 * sq_relu_mlp(hc2, w1[l], w2[l])

        x = x + g1 * y
        h2 = modulate(rmsnorm(x, norm2_g[l]), sh2, sc2)
        x = x + g2 * sq_relu_mlp(h2, w1[l], w2[l])
    return rmsnorm(x, final_norm_g)


_drawn_inputs = setup_inputs


def setup_inputs(seed=0):
    import zlib

    import numpy as np

    out = dict(_drawn_inputs(seed))
    spreads = {}
    factors = {'ctx': 6.324,
     'norm1_g': 8.0,
     'q_norm_g': 8.0,
     'k_norm_g': 8.0,
     'norm2_g': 5.904,
     'final_norm_g': 2.914}
    for name, (base, spread) in spreads.items():
        noise = np.random.default_rng([zlib.crc32(name.encode()), seed]).standard_normal(out[name].shape)
        drawn = base * np.exp(spread * noise) if base else spread * noise
        out[name] = jnp.asarray(drawn.astype(out[name].dtype))
    for name, factor in factors.items():
        out[name] = (out[name] * factor).astype(out[name].dtype)
    return out
```

```python
from contextlib import ExitStack

import numpy as np

import concourse.bass as bass
from concourse import mybir

F32 = mybir.dt.float32
F32R = mybir.dt.float32r
ALU = mybir.AluOpType
ACT = mybir.ActivationFunctionType
AX = mybir.AxisListType

P = 128
D = 2048
T = 256
TB = T // P
KT = D // P
HD = 128
NH = 16
NKV = 4
QPK = NH // NKV
DFF = 4 * D
FW = 1024
FG = 256
NC = 1024
HC = 512
EPS = 1e-6
SCALE = HD ** -0.5
K0, V0, FO0, GA0, GF0 = 2048, 2560, 3072, 4096, 6144

RAW = 4
SPL = 4
AHEAD = 2

CHUNKS = [("K", 8), ("V", 8), ("F", 16), ("Q0", 16), ("Q1", 16), ("GA0", 16), ("GA1", 16),
          ("GF0", 16), ("GF1", 16), ("A0", 16), ("B0", 8), ("A1", 16), ("B1", 8), ("O0", 16), ("O1", 16)]
CI = {name: i for i, (name, _) in enumerate(CHUNKS)}
FIRST, LAST, TILES = {}, {}, []
for _name, _n in CHUNKS:
    FIRST[_name] = len(TILES)
    TILES += [(_name, k) for k in range(_n)]
    LAST[_name] = len(TILES) - 1
M1 = len(TILES)
N1 = DFF // NC
M2 = M1 + N1 * KT
N2 = DFF // P * (D // NC)
CI1 = len(CHUNKS)

ADA_COLS = [6, 7, 8, 9, 4, 5, 10, 11]
P0_KINDS = [(0, 0), (1, 0), (0, 1), (1, 1)]
P0_DVE = (1, 3, 5, 7, 9, 11, 13)
STREAM = [("P0", p, k) for p in range(4) for k in range(KT)]
ADA_AT = {}
ADA_END = {}
_units, _n = 0.0, 0
for _m, (_name, _k) in enumerate(TILES):
    STREAM.append(("M", _m, 0))
    _units += 2.0 if _name in "KV" else 1.0
    ADA_AT[_m] = []
    while _n < 128 and _n < _units * 0.585:
        ADA_AT[_m].append(_n)
        STREAM.append(("A", _n // KT, _n % KT))
        if _n % KT == KT - 1:
            ADA_END[_m] = _n // KT
        _n += 1
assert _n == 128
S1 = len(STREAM)
STREAM_AT = {("M", m): i for i, (kind, m, _) in enumerate(STREAM) if kind == "M"}

FOUR1 = {FIRST["Q0"] + 1 + d: d for d in range(8)}
FOUR2 = {FIRST["Q0"] + 9 + g: g for g in range(4)}
KTR = {FIRST["V"] + 6 + t: t for t in range(4)}
ROPE_Q = {FIRST[f"Q{c}"] + 17 + g: (c, g) for c in range(2) for g in range(4)}
QTR = {FIRST[f"Q{c}"] + 19 + g: (c, g) for c in range(2) for g in range(4)}
UNITS = NH * TB
SLOT0 = FIRST["Q1"] + 8
SLOTS = {SLOT0 + 2 * u: u for u in range(UNITS + 3)}
OH = {SLOT0 + 2 * UNITS + 1 + g: g for g in range(4)}
OL = {SLOT0 + 2 * (UNITS + 2) + g: g for g in range(4)}
MTR = {FIRST["B0"] + 10 + g: (0, g) for g in range(4)} | {FIRST["O0"] + 1 + g: (1, g) for g in range(4)}
XS_NOW = 3
G1_LOAD, G2_LOAD, X_LOAD = FIRST["Q0"] + 24, FIRST["A0"] + 4, FIRST["A1"] + 20
ADA_SUM = {m + 1: jc for m, jc in ADA_END.items()}
ADA_SUM = {min(m, M1 - 1): jc for m, jc in ADA_SUM.items()}

MISC = [("vec", 0)]
for _p in range(4):
    if _p in (1, 2):
        MISC += [(("x", "c")[_p - 1], g) for g in range(8)]
    MISC.append(("mod", _p))
for _m in range(M1):
    if _m in ADA_SUM:
        MISC += [("ada", ADA_SUM[_m], h) for h in range(1 if ADA_SUM[_m] < 4 else 2)]
    if _m in KTR:
        MISC.append(("k", KTR[_m]))
    if _m in FOUR1:
        MISC.append(("four1", FOUR1[_m]))
    if _m in FOUR2:
        MISC.append(("four2", FOUR2[_m]))
    if _m in QTR:
        MISC.append(("q", QTR[_m]))
    if _m in MTR:
        MISC.append(("m", MTR[_m]))
MISC += [("xs", g) for g in range(8)]
MISC_AT, _uses = {}, {4: 0, 5: 0, 6: 0, 7: 0}
_busy_from = next(i for i, k in enumerate(MISC) if k == ("q", (0, 3))) + 1
_busy_to = next(i for i, k in enumerate(MISC) if k == ("m", (0, 0)))
_turn = 0
for _i, _key in enumerate(MISC):
    if _busy_from <= _i < _busy_to:
        _b = 5
    else:
        _b = (5, 6, 7)[_turn % 3]
        _turn += 1
    MISC_AT[_key] = (_b, _uses[_b])
    _uses[_b] += 1

HI = [("f", g) for g in range(4)] + [("o", g) for g in range(4)]
HI += [("m", k) for k in MTR.values()] + [("xs", k) for k in range(KT)]
HI_AT = {key: i + 1 for i, key in enumerate(HI)}


def block_program(nc, x, c, ctx_, c_ctx, w_ada, b_ada, norm1_g, w_in, q_norm_g, k_norm_g,
                  w_attn_o, w_fourier, w_out, norm2_g, w1, w2, final_norm_g,
                  identity, dft, rope_c, rope_s, out):
    with ExitStack() as stack:
        base = (nc.sbuf_base + 63) // 64 * 64
        where = {}
        at = base
        for region, size in [("raw", 16), ("wh", 16), ("wl", 16), ("acc", 8), ("h", 32), ("x", 16), ("c", 32),
                             ("q", 16), ("kv", 16), ("f", 16), ("p", 8), ("g1", 8)]:
            where[region] = at
            at += size * 1024
        small = [at]

        def place(name, shape, dt, region, skip=0):
            return nc.alloc_sbuf_tensor_at(name, shape, dt, offset=where[region] + skip)

        def little(name, shape, dt=F32):
            t = nc.alloc_sbuf_tensor_at(name, shape, dt, offset=small[0])
            n = 4
            for d in shape[1:]:
                n *= d
            small[0] += (n + 31) // 32 * 32
            return t

        raw = place("raw", [P, RAW, NC], F32, "raw")
        wh = place("wh", [P, SPL, NC], F32R, "wh")
        wl = place("wl", [P, SPL, NC], F32R, "wl")
        acc = place("acc", [P, 2, NC], F32, "acc")
        hT = [place(f"hT{i}", [P, KT, T], F32R, "h", i * 16384) for i in range(2)]
        cT = [place(f"cT{i}", [P, KT, T], F32R, "c", i * 16384) for i in range(2)]
        oS = [place("oS0", [P, KT, T], F32R, "q"), place("oS1", [P, KT, T], F32R, "kv")]
        mT = [place(f"mT{i}", [P, KT, T], F32R, "h", i * 16384) for i in range(2)]
        h2T = [place(f"h2T{i}", [P, KT, T], F32R, "h", i * 16384) for i in range(2)]
        yT = [place(f"yT{i}", [P, FW // P, T], F32R, "f", i * 8192) for i in range(2)]
        hidS = [place(f"hidS{i}", [P, 2, 2, T], F32R, "f", 8192 + i * 4096) for i in range(2)]
        xt = place("xt", [P, TB, D], F32, "x")
        ct = place("ct", [P, TB, D], F32, "kv")
        junk_x = place("junk_x", [P, D], F32, "h")
        xhT = place("xhT", [P, KT, T], F32, "q")
        chT = place("chT", [P, KT, T], F32, "f")
        modrow = place("modrow", [2, NC], F32, "p")
        hmod = place("hmod", [P, 2, 2, T], F32, "p", 4096)
        kraw = place("kraw", [P, 4, HC], F32, "x")
        krot = place("krot", [P, 4, HC], F32, "x", 8192)
        kT = place("kT", [P, NKV, 2 * T], F32, "kv")
        v = place("v", [P, 2 * TB, HC], F32, "kv", 8192)
        fin = place("fin", [P, TB, FW], F32, "f")
        ab = place("ab", [P, FW // P, 2 * T], F32, "x")
        qraw = place("qraw", [P, TB, NC], F32, "x")
        qrot = place("qrot", [P, TB, NC], F32, "x", 8192)
        qT = place("qT", [P, NH, T], F32, "q")
        probs = place("probs", [P, 2, 2 * T], F32, "p")
        probsT = place("probsT", [P, 2, 4, P], F32, "p", 4096)
        oT = place("oT", [P, NH, T], F32, "c")
        gateA = place("gateA", [P, TB, D], F32, "x")
        gateF = place("gateF", [P, TB, D], F32, "c", 16384)
        x1 = place("x1", [P, TB, D], F32, "kv")
        scr = place("scr", [P, 4, HC], F32, "f")
        junk_1 = place("junk_1", [P, 4, HC], F32, "f", 8192)
        xs = place("xs", [P, TB, D], F32, "x")
        hs = place("hs", [P, TB, NC], F32, "f")
        hmod2 = place("hmod2", [P, 2, 2, T], F32, "acc")
        hid = place("hid", [P, DFF // P, T], F32, "x")
        g1row = place("g1row", [P, D], F32, "g1")
        dft_sb = place("dft_sb", [P, TB, 3 * FG], F32, "g1")
        g2row = place("g2row", [P, D], F32, "p")
        fgrow = place("fgrow", [P, D], F32, "g1")
        scr2 = place("scr2", [P, 8, HC], F32, "h")
        junk_2 = place("junk_2", [P, 8, HC], F32, "h", 16384)
        res = place("res", [P, TB, D], F32, "x")
        ident = little("ident", [P, P])
        ones = little("ones", [P, P])
        pick = little("pick", [P, 2, 2])
        rows = little("rows", [P, P])
        cols = little("cols", [P, P])
        th = little("th", [P, 2, KT])
        cc = little("cc", [P, KT, 2])
        mods = little("mods", [P, 2, KT, 2])
        gain1 = little("gain1", [P, KT, 2])
        mods2 = little("mods2", [P, 2, KT])
        gain2 = little("gain2", [P, KT])
        ropeC = little("ropeC", [P, TB, HD])
        ropeS = little("ropeS", [P, TB, HD])
        tabC = little("tabC", [P, TB, HD])
        tabS = little("tabS", [P, TB, HD])
        gq = little("gq", [P, 2, HD])
        ssx = little("ssx", [P, 4])
        ssk = little("ssk", [P, 16])
        ssq = little("ssq", [P, 2, 16])
        ss1 = little("ss1", [P, TB, 4])
        ss2 = little("ss2", [P, TB, 4])
        msum = little("msum", [P, 16])
        msum2 = little("msum2", [P, 4])
        half_neg = little("half_neg", [P, 16])
        rsx = little("rsx", [P, 4])
        rsk = little("rsk", [P, 16])
        rsq = little("rsq", [P, 2, 16])
        qs = little("qs", [P, 2, 16])
        nqs = little("nqs", [P, 2, 16])
        rs1 = little("rs1", [P, TB])
        rs2 = little("rs2", [P, TB])
        mx = little("mx", [P, UNITS])
        nb = little("nb", [P, UNITS])
        rsum = little("rsum", [P, UNITS])
        rinv = little("rinv", [P, UNITS])
        assert small[0] <= nc.sbuf_usable_end, (small[0], nc.sbuf_usable_end)

        bank = [stack.enter_context(nc.psum_tensor(f"bank{i}", [P, HC], F32)) for i in range(8)]

        def sem(name):
            return stack.enter_context(nc.semaphore(name))

        vec_in = sem("vec_in")
        x_in = sem("x_in")
        ctx_in = sem("ctx_in")
        ident_in = sem("ident_in")
        dft_in = sem("dft_in")
        rope_in = sem("rope_in")
        raw_full = [sem(f"raw_full{i}") for i in range(RAW)]
        g1_in = sem("g1_in")
        g2_in = sem("g2_in")
        xr_in = sem("xr_in")
        fg_in = sem("fg_in")
        stored = sem("stored")
        const_set = sem("const_set")
        pool_step = sem("pool_step")
        dve_step = sem("dve_step")
        tanh_ready = sem("tanh_ready")
        cc_ready = sem("cc_ready")
        acc_step = sem("acc_step")
        p0_mm = sem("p0_mm")
        p0_sum = sem("p0_sum")
        modrow_ready = sem("modrow_ready")
        sqx_ready = sem("sqx_ready")
        rstd_ready = sem("rstd_ready")
        xn_ready = sem("xn_ready")
        gain_ready = sem("gain_ready")
        h_hi = sem("h_hi")
        h_tmp = sem("h_tmp")
        h_lo = sem("h_lo")
        wh_done = sem("wh_done")
        wl_done = sem("wl_done")
        gemm_done = sem("gemm_done")
        bank_full = sem("bank_full")
        bank_free = sem("bank_free")
        misc_full = {b: sem(f"misc_full{b}") for b in (5, 6, 7)}
        misc_free = {b: sem(f"misc_free{b}") for b in (5, 6, 7)}
        mac_step = sem("mac_step")
        g_done = sem("g_done")
        sqk_ready = sem("sqk_ready")
        sqq_ready = sem("sqq_ready")
        kn_ready = sem("kn_ready")
        qr_ready = sem("qr_ready")
        hi_done = sem("hi_done")
        s_done = sem("s_done")
        nb_ready = sem("nb_ready")
        exp_done = sem("exp_done")
        pn_ready = sem("pn_ready")
        pt_full = sem("pt_full")
        pt_ready = sem("pt_ready")
        pv_done = sem("pv_done")
        o_ready = sem("o_ready")
        ol_done = sem("ol_done")
        mid_done = sem("mid_done")
        x1_ready = sem("x1_ready")
        sq1_ready = sem("sq1_ready")
        xs_ready = sem("xs_ready")
        hT_full = sem("hT_full")
        hid_ready = sem("hid_ready")
        hs_hi = sem("hs_hi")
        hs_lo = sem("hs_lo")
        x2_ready = sem("x2_ready")
        sq2_ready = sem("sq2_ready")
        res_ready = sem("res_ready")

        block = stack.enter_context(nc.Block())

        def misc_wait_full(eng, key):
            b, n = MISC_AT[key]
            eng.wait_ge(misc_full[b], n + 1)
            return bank[b]

        def misc_wait_freed(eng, key):
            b, n = MISC_AT[key]
            eng.wait_ge(misc_free[b], n + 1)

        def wait_bank(eng, ci, last, b):
            if b < 3:
                eng.wait_ge(bank_full, 3 * ci + b + 1)
            else:
                eng.wait_ge(gemm_done, last + 1)

        @block.sync
        def _(sp):
            def slot_free(s):
                if s < RAW:
                    return
                kind, a, k = STREAM[s - RAW]
                if kind == "P0" and k in P0_DVE:
                    sp.wait_ge(acc_step, (a * len(P0_DVE) + P0_DVE.index(k) + 1) * 2)
                elif kind == "P0":
                    sp.wait_ge(p0_mm, a * (KT - len(P0_DVE)) + sum(j not in P0_DVE for j in range(k + 1)))
                elif kind == "M":
                    sp.wait_ge(wl_done, a + 1)
                else:
                    sp.wait_ge(mac_step, a * KT + k + 1)

            def tile_source(m):
                name, k = TILES[m]
                r = slice(k * P, (k + 1) * P)
                if name in "KV":
                    col = K0 if name == "K" else V0
                    return w_in[2 * k * P:2 * (k + 1) * P, col:col + HC].rearrange("(t p) n -> p t n", p=P)
                col0 = {"F": FO0, "Q0": 0, "Q1": NC, "GA0": GA0, "GA1": GA0 + NC, "GF0": GF0, "GF1": GF0 + NC}
                if name in col0:
                    return w_in[r, col0[name]:col0[name] + NC]
                n = int(name[1])
                return {"A": w_attn_o, "B": w_fourier, "O": w_out}[name[0]][r, n * NC:(n + 1) * NC]

            for s, (kind, a, k) in enumerate(STREAM):
                if kind == "M" and a == G1_LOAD:
                    b, n = MISC_AT["four2", 3]
                    sp.wait_ge(misc_full[b], n + 1)
                    sp.dma_start(g1row[:], b_ada[2 * D:3 * D].partition_broadcast(P)).then_inc(g1_in, 16)
                if kind == "M" and a == G2_LOAD:
                    sp.wait_ge(pv_done, UNITS)
                    sp.dma_start(g2row[:], b_ada[5 * D:6 * D].partition_broadcast(P)).then_inc(g2_in, 16)
                if kind == "M" and a == X_LOAD:
                    sp.wait_ge(gemm_done, LAST["A1"] + 1)
                    sp.dma_start(x1[:], x.rearrange("(b p) n -> p b n", p=P)).then_inc(xr_in, 16)
                slot_free(s)
                if kind == "M":
                    src = tile_source(a)
                else:
                    chunk = P0_KINDS[a][0] * 2 + P0_KINDS[a][1] if kind == "P0" else ADA_COLS[a]
                    src = w_ada[k * P:(k + 1) * P, chunk * NC:(chunk + 1) * NC]
                dst = raw[:, s % RAW, :]
                if kind == "M" and TILES[a][0] in "KV":
                    dst = dst.rearrange("p (t n) -> p t n", t=2)
                sp.dma_start(dst, src).then_inc(raw_full[s % RAW], 16)

            def load_w1(i, k):
                s = S1 + k
                if isinstance(i, int) and i == 0 and k < RAW:
                    slot_free(s)
                else:
                    sp.wait_ge(wl_done, i * KT + (M1 + k - RAW + 1))
                sp.dma_start(raw[:, s % RAW, :], w1[k * P:(k + 1) * P, bass.ts(i, NC)])\
                    .then_inc(raw_full[s % RAW], 16)

            for k in range(KT):
                load_w1(0, k)
            with nc.sync.Fori(1, N1) as i:
                for k in range(KT):
                    load_w1(i, k)
            with nc.sync.Fori(0, N2 // 8) as g:
                for j in range(8):
                    sp.wait_ge(wl_done, g * 8 + (M2 + j - RAW + 1))
                    sp.dma_start(raw[:, (S1 + j) % RAW, :],
                                 w2[bass.ds(g * 512 + (j // 2) * P, P), (j % 2) * NC:(j % 2 + 1) * NC])\
                        .then_inc(raw_full[(S1 + j) % RAW], 16)
            sp.wait_ge(x1_ready, 8)
            sp.dma_start(fgrow[:], final_norm_g.partition_broadcast(P)).then_inc(fg_in, 16)
            for b in range(TB):
                sp.wait_ge(res_ready, b + 1)
                sp.dma_start(out[b * P:(b + 1) * P, :], res[:, b, :]).then_inc(stored, 16)
            sp.wait_ge(stored, 16 * TB)

        @block.gpsimd
        def _(pool):
            nc.gpsimd.memset(ones[:], 1.0).then_inc(const_set, 1)
            nc.gpsimd.memset(pick[:], 0.0).then_inc(const_set, 1)
            nc.gpsimd.memset(half_neg[:], -0.5).then_inc(const_set, 1)
            pool.wait_ge(const_set, 3)
            nc.gpsimd.memset(pick[:, 0, 0:1], 1.0).then_inc(const_set, 1)
            nc.gpsimd.memset(pick[:, 1, 1:2], 1.0).then_inc(const_set, 1)
            steps = [0]

            def then(ins):
                steps[0] += 1
                ins.then_inc(pool_step, 1)
                pool.wait_ge(pool_step, steps[0])

            def rstd(result, total, mean, width, n):
                then(nc.gpsimd.tensor_scalar(mean, total, 1.0 / width, EPS, ALU.mult, ALU.add))
                return nc.gpsimd.tensor_tensor(result, mean, half_neg[:, 0:n], ALU.pow)

            pool.wait_ge(sqx_ready, 4)
            rstd(rsx[:], ssx[:], msum[:, 0:4], D, 4).then_inc(rstd_ready, 1)
            pool.wait_ge(sqk_ready, 16)
            pool.wait_ge(rstd_ready, 1)
            rstd(rsk[:], ssk[:], msum[:], HD, 16).then_inc(rstd_ready, 1)
            for ch in range(2):
                pool.wait_ge(sqq_ready, 16 * (ch + 1))
                pool.wait_ge(rstd_ready, 2 + ch)
                then(rstd(rsq[:, ch, :], ssq[:, ch, :], msum[:], HD, 16))
                then(nc.gpsimd.tensor_scalar(qs[:, ch, :], rsq[:, ch, :], SCALE, None, ALU.mult))
                nc.gpsimd.tensor_scalar(nqs[:, ch, :], qs[:, ch, :], -1.0, None, ALU.mult).then_inc(rstd_ready, 1)
            for parts, result, seen, n in ((ss1, rs1, sq1_ready, 4), (ss2, rs2, sq2_ready, 5)):
                pool.wait_ge(seen, 8)
                pool.wait_ge(rstd_ready, n)
                then(nc.gpsimd.tensor_tensor(parts[:, :, 0:2], parts[:, :, 0:2], parts[:, :, 2:4], ALU.add))
                then(nc.gpsimd.tensor_tensor(msum2[:, 0:2], parts[:, :, 0], parts[:, :, 1], ALU.add))
                rstd(result[:], msum2[:, 0:2], msum2[:, 2:4], D, 2).then_inc(rstd_ready, 1)

        @block.scalar
        def _(act):
            act.dma_start(ident[:], identity).then_inc(ident_in, 16)
            act.dma_start(rows[0:16, :], c.rearrange("(r n) -> r n", n=P)).then_inc(vec_in, 16)
            act.dma_start(rows[16:32, :], c_ctx.rearrange("(r n) -> r n", n=P)).then_inc(vec_in, 16)
            act.dma_start(rows[32:48, :], norm1_g.rearrange("(r n) -> r n", n=P)).then_inc(vec_in, 16)
            act.dma_start(rows[48:64, :], norm2_g.rearrange("(r n) -> r n", n=P)).then_inc(vec_in, 16)
            act.dma_start(rows[64:96, :], b_ada[0:2 * D].rearrange("(r n) -> r n", n=P)).then_inc(vec_in, 16)
            act.dma_start(rows[96:128, :], b_ada[3 * D:5 * D].rearrange("(r n) -> r n", n=P)).then_inc(vec_in, 16)
            act.dma_start(xt[:], x.rearrange("(b p) n -> p b n", p=P)).then_inc(x_in, 16)
            act.dma_start(ct[:], ctx_.rearrange("(b p) n -> p b n", p=P)).then_inc(ctx_in, 16)
            act.dma_start(ropeC[:], rope_c.rearrange("(b p) n -> p b n", p=P)).then_inc(rope_in, 16)
            act.dma_start(ropeS[:], rope_s.rearrange("(b p) n -> p b n", p=P)).then_inc(rope_in, 16)
            act.dma_start(gq[:, 0, :], q_norm_g.partition_broadcast(P)).then_inc(rope_in, 16)
            act.dma_start(gq[:, 1, :], k_norm_g.partition_broadcast(P)).then_inc(rope_in, 16)
            act.dma_start(dft_sb[:], dft.rearrange("(b p) n -> p b n", p=P)).then_inc(dft_in, 16)

            b0 = misc_wait_full(act, ("vec", 0))
            nc.scalar.activation(cols[:], b0[:, 0:P], ACT.Copy).then_inc(misc_free[MISC_AT["vec", 0][0]], 1)
            misc_wait_freed(act, ("vec", 0))
            nc.scalar.activation(th[:], cols[:, 0:2 * KT].rearrange("p (v k) -> p v k", v=2), ACT.Tanh, scale=0.5)\
                .then_inc(tanh_ready, 1)
            for n, (t, arrived) in enumerate([(xt, x_in), (xt, x_in), (ct, ctx_in), (ct, ctx_in)]):
                act.wait_ge(arrived, 16)
                if n:
                    act.wait_ge(sqx_ready, n)
                nc.scalar.activation(junk_x[:], t[:, n % 2, :], ACT.Square, accum_out=ssx[:, n:n + 1])\
                    .then_inc(sqx_ready, 1)

            def modrows(p):
                act.wait_ge(p0_sum, p + 1)
                if p:
                    misc_wait_full(act, ("mod", p - 1))
                for half in range(2):
                    nc.scalar.activation(modrow[:, half * HC:(half + 1) * HC], bank[2 * (p % 2) + half][0:2, :], ACT.Copy)\
                        .then_inc(modrow_ready, 1)

            for p in range(4):
                if p in (1, 2):
                    for g in range(8):
                        key = (("x", "c")[p - 1], g)
                        b = misc_wait_full(act, key)
                        nc.scalar.activation((xhT, chT)[p - 1][:, 2 * g:2 * g + 2, :].rearrange("p f t -> p (f t)"),
                                             b[:], ACT.Copy).then_inc(misc_free[MISC_AT[key][0]], 1)
                modrows(p)

            def split_hi(m_wait, slot_wait, s, m, n_raw):
                act.wait_ge(raw_full[s % RAW], n_raw)
                if slot_wait is not None:
                    act.wait_ge(gemm_done, slot_wait)
                nc.scalar.activation(wh[:, m % SPL, :], raw[:, s % RAW, :], ACT.Copy).then_inc(wh_done, 1)

            def modulate_hi(k):
                act.wait_ge(gain_ready, 1 if k < 4 else 2)
                for src, dst, vv in ((xhT, hT, 0), (chT, cT, 1)):
                    misc_wait_freed(act, (("x", "c")[vv], k))
                    for f in (2 * k, 2 * k + 1):
                        nc.scalar.activation(dst[0][:, f, :], src[:, f, :], ACT.Identity,
                                             bias=mods[:, 0, f, vv:vv + 1], scale=gain1[:, f, vv:vv + 1])\
                            .then_inc(h_hi, 1)

            def evacuate(name, func, dest, **kw):
                for b in range(4):
                    wait_bank(act, CI[name], LAST[name], b)
                    nc.scalar.activation(dest(b), bank[b][:], func, **kw).then_inc(bank_free, 1)

            def cut(t, col):
                return lambda b: t[:, b % 2, col + b // 2 * HC:col + (b // 2 + 1) * HC]

            def squares(src, total, seen, n):
                for h in range(4):
                    if n + h:
                        act.wait_ge(seen, n + h)
                    nc.scalar.activation(rows[:], src(h), ACT.Square, accum_out=total(h)).then_inc(seen, 1)

            def post(m):
                name, k = TILES[m]
                if m == LAST["K"]:
                    misc_wait_freed(act, ("x", 7))
                    evacuate("K", ACT.Copy, lambda b: kraw[:, b, :])
                if 0 <= m - LAST["K"] - 1 < 4:
                    t = m - LAST["K"] - 1
                    if t == 0:
                        act.wait_ge(bank_free, 4 * CI["K"] + 4)
                        act.wait_ge(const_set, 5)
                    squares(lambda h: kraw[:, t, h * HD:(h + 1) * HD], lambda h: ssk[:, 4 * t + h:4 * t + h + 1],
                            sqk_ready, 4 * t)
                if m == LAST["V"]:
                    misc_wait_freed(act, ("c", 7))
                    evacuate("V", ACT.Copy, lambda b: v[:, b, :])
                if m in KTR:
                    t = KTR[m]
                    b = misc_wait_full(act, ("k", t))
                    nc.scalar.activation(kT[:, :, t * P:(t + 1) * P], b[:].rearrange("p (h t) -> p h t", h=NKV),
                                         ACT.Copy).then_inc(misc_free[MISC_AT["k", t][0]], 1)
                if m == LAST["F"]:
                    evacuate("F", ACT.Copy, cut(fin, 0))
                if m in FOUR1:
                    d = FOUR1[m]
                    b = misc_wait_full(act, ("four1", d))
                    nc.scalar.activation(ab[:, d, :], b[:], ACT.Copy).then_inc(misc_free[MISC_AT["four1", d][0]], 1)
                if m in FOUR2:
                    g = FOUR2[m]
                    b = misc_wait_full(act, ("four2", g))
                    nc.scalar.activation(yT[0][:, 2 * g:2 * g + 2, :].rearrange("p f t -> p (f t)"), b[:], ACT.Copy)\
                        .then_inc(hi_done, 1)
                for ch in range(2):
                    if m == LAST[f"Q{ch}"]:
                        if ch:
                            act.wait_ge(qr_ready, 4)
                        evacuate(f"Q{ch}", ACT.Copy, cut(qraw, 0))
                    g = m - LAST[f"Q{ch}"] - 1
                    if 0 <= g < 4:
                        if g == 0:
                            act.wait_ge(bank_free, 4 * CI[f"Q{ch}"] + 4)
                            if ch == 0:
                                act.wait_ge(sqk_ready, 16)
                        squares(lambda h: qraw[:, g // 2, (g % 2 * 4 + h) * HD:(g % 2 * 4 + h + 1) * HD],
                                lambda h: ssq[:, ch, 4 * g + h:4 * g + h + 1], sqq_ready, 16 * ch + 4 * g)
                if m in QTR:
                    ch, g = QTR[m]
                    b = misc_wait_full(act, ("q", (ch, g)))
                    h0 = 8 * ch + g % 2 * 4
                    nc.scalar.activation(qT[:, h0:h0 + 4, g // 2 * P:(g // 2 + 1) * P],
                                         b[:].rearrange("p (h t) -> p h t", h=4), ACT.Copy)\
                        .then_inc(misc_free[MISC_AT["q", (ch, g)][0]], 1)
                if m in SLOTS:
                    u = SLOTS[m]
                    if u < UNITS:
                        h, t = divmod(u, TB)
                        col = 8 * t + h % 8
                        act.wait_ge(nb_ready, u + 1)
                        if u >= 2:
                            act.wait_ge(pt_full, u - 1)
                        nc.scalar.activation(probs[:, u % 2, :], bank[4][:], ACT.Exp, bias=nb[:, u:u + 1],
                                             scale=qs[:, h // 8, col:col + 1], accum_out=rsum[:, u:u + 1])\
                            .then_inc(exp_done, 1)
                    if 2 <= u < UNITS + 2:
                        w = u - 2
                        act.wait_ge(pt_full, w + 1)
                        if w >= 2:
                            act.wait_ge(pv_done, w - 1)
                        nc.scalar.activation(probsT[:, w % 2, :, :].rearrange("p k q -> p (k q)"), bank[6][:], ACT.Copy)\
                            .then_inc(pt_ready, 1)
                    if 3 <= u:
                        w = u - 3
                        h, t = divmod(w, TB)
                        act.wait_ge(pv_done, w + 1)
                        nc.scalar.activation(oT[:, h, t * P:(t + 1) * P], bank[7][:, 0:P], ACT.Copy)\
                            .then_inc(o_ready, 1)
                for ch in range(2):
                    if m == LAST[f"GA{ch}"]:
                        if ch == 0:
                            misc_wait_full(act, ("q", (1, 3)))
                        evacuate(f"GA{ch}", ACT.Tanh, cut(gateA, ch * NC), scale=0.5)
                    if m == LAST[f"GF{ch}"]:
                        evacuate(f"GF{ch}", ACT.Tanh, cut(gateF, ch * NC), scale=0.5)
                if m in OH:
                    g = OH[m]
                    act.wait_ge(s_done, UNITS)
                    act.wait_ge(o_ready, 8 * (g + 1))
                    nc.scalar.activation(oS[0][:, 4 * g:4 * g + 4, :], oT[:, 4 * g:4 * g + 4, :], ACT.Copy)\
                        .then_inc(hi_done, 1)
                if m in MTR:
                    ch, g = MTR[m]
                    b = misc_wait_full(act, ("m", (ch, g)))
                    f = 8 * ch + 2 * g
                    nc.scalar.activation(mT[0][:, f:f + 2, :].rearrange("p f t -> p (f t)"), b[:], ACT.Copy, scale=0.5)\
                        .then_inc(hi_done, 1)
                for ch in range(2):
                    if m == LAST[f"O{ch}"]:
                        for b in range(4):
                            n = 4 * ch + b
                            act.wait_ge(x1_ready, n + 1)
                            if n:
                                act.wait_ge(sq1_ready, n)
                            nc.scalar.activation(junk_1[:, b, :], cut(x1, ch * NC)(b), ACT.Square,
                                                 accum_out=ss1[:, b % 2, 2 * ch + b // 2:2 * ch + b // 2 + 1])\
                                .then_inc(sq1_ready, 1)

            def modulate2_hi(g):
                b = misc_wait_full(act, ("xs", g))
                for j in range(2):
                    f = 2 * g + j
                    nc.scalar.activation(h2T[0][:, f, :], b[:, j * T:(j + 1) * T], ACT.Identity,
                                         bias=mods2[:, 0, f:f + 1], scale=gain2[:, f:f + 1]).then_inc(hi_done, 1)

            for m, (name, k) in enumerate(TILES):
                if name == "K":
                    modulate_hi(k)
                s = STREAM_AT["M", m]
                split_hi(m, m - SPL + 1 if m >= SPL else None, s, m, 16 * (s // RAW + 1))
                if m >= AHEAD:
                    post(m - AHEAD)

            def hi_1(i, k):
                s = S1 + k
                split_hi(None, i * KT + (M1 + k - SPL + 1), s, k, i * (16 * KT // RAW) + 16 * (s // RAW + 1))

            def hidden(i, g):
                act.wait_ge(hT_full, i * 4 + (g + 1))
                nc.scalar.activation(hid[:, bass.ds(i * 8 + 2 * g, 2), :], bank[4 + g][:].rearrange("p (f t) -> p f t", f=2),
                                     ACT.Square).then_inc(hid_ready, 1)

            for k in range(KT):
                hi_1(0, k)
                if k < AHEAD:
                    post(M1 - AHEAD + k)
                if k == AHEAD - 1:
                    for g in range(XS_NOW):
                        modulate2_hi(g)
                if AHEAD <= k and XS_NOW + k - AHEAD < 8:
                    modulate2_hi(XS_NOW + k - AHEAD)
            with nc.scalar.Fori(1, N1) as i:
                for k in range(KT):
                    hi_1(i, k)
                    if 3 <= k < 7:
                        hidden(i - 1, k - 3)

            def hi_2(g, j):
                s = S1 + j
                if j % 4 == 0:
                    q = j // 4
                    if not (isinstance(g, int) and g == 0):
                        act.wait_ge(gemm_done, g * 8 + (M2 + j - 4))
                    nc.scalar.activation(hidS[0][:, q, :, :], hid[:, bass.ds(g * 4 + 2 * q, 2), :], ACT.Copy)\
                        .then_inc(hs_hi, 1)
                split_hi(None, g * 8 + (M2 + j - SPL + 1), s, j,
                         g * (16 * 8 // RAW) + 16 * ((s + (M2 - M1)) // RAW + 1))

            for j in range(8):
                hi_2(0, j)
                if j == 1:
                    for g in range(4):
                        hidden(N1 - 1, g)
            with nc.scalar.Fori(1, N2 // 8) as g:
                for j in range(8):
                    hi_2(g, j)
            for b in range(8):
                n, half, t = b // 4, b // 2 % 2, b % 2
                act.wait_ge(x2_ready, b + 1)
                if b:
                    act.wait_ge(sq2_ready, b)
                nc.scalar.activation(junk_2[:, b, :], x1[:, t, n * NC + half * HC:n * NC + (half + 1) * HC], ACT.Square,
                                     accum_out=ss2[:, t, 2 * n + half:2 * n + half + 1]).then_inc(sq2_ready, 1)

        @block.vector
        def _(dve):
            steps = [0]

            def then(ins):
                steps[0] += 1
                ins.then_inc(dve_step, 1)
                dve.wait_ge(dve_step, steps[0])

            dve.wait_ge(tanh_ready, 1)
            then(nc.vector.tensor_scalar(th[:], th[:], 1.0, 0.5, ALU.add, ALU.mult))
            nc.vector.tensor_tensor(cc[:].rearrange("p k v -> p v k"), th[:],
                                    cols[:, 0:2 * KT].rearrange("p (v k) -> p v k", v=2), ALU.mult).then_inc(cc_ready, 1)
            dve.wait_ge(cc_ready, 1)

            def rope_tables(which):
                pair = gq[:, which, :].rearrange("p (j two) -> p j two", two=2)
                for t in range(TB):
                    then(nc.vector.tensor_tensor(tabC[:, t, :], ropeC[:, t, :], gq[:, which, :], ALU.mult))
                    s_in = ropeS[:, t, :].rearrange("p (j two) -> p j two", two=2)
                    s_out = tabS[:, t, :].rearrange("p (j two) -> p j two", two=2)
                    for e in range(2):
                        then(nc.vector.tensor_tensor(s_out[:, :, e], s_in[:, :, e], pair[:, :, 1 - e], ALU.mult))

            def p0_chunk(p):
                for i, k in enumerate(P0_DVE):
                    s = p * KT + k
                    dve.wait_ge(raw_full[s % RAW], 16 * (s // RAW + 1))
                    if i == 0 and p:
                        dve.wait_ge(p0_sum, p)
                    for vv in range(2):
                        n = (p * len(P0_DVE) + i) * 2 + vv
                        if i == 0:
                            nc.vector.tensor_scalar(acc[:, vv, :], raw[:, s % RAW, :], cc[:, k, vv:vv + 1], None, ALU.mult)\
                                .then_inc(acc_step, 1)
                        else:
                            dve.wait_ge(acc_step, n - 1)
                            nc.vector.scalar_tensor_tensor(acc[:, vv, :], raw[:, s % RAW, :], cc[:, k, vv:vv + 1],
                                                           acc[:, vv, :], ALU.mult, ALU.add).then_inc(acc_step, 1)
                    if i == 0 and p:
                        mod_columns(p - 1)

            def mod_columns(p):
                kind, half = P0_KINDS[p]
                b = misc_wait_full(dve, ("mod", p))
                f = slice(8 * half, 8 * half + 8)
                bias = cols[:, 64 + 16 * kind + 8 * half:72 + 16 * kind + 8 * half]
                mine = b[:, 0:16].rearrange("p (f v) -> p f v", v=2)
                for vv in range(2):
                    ins = nc.vector.tensor_tensor(mods[:, kind, f, vv], mine[:, :, vv], bias, ALU.add)
                    if vv == 0:
                        then(ins)
                ins.then_inc(misc_free[MISC_AT["mod", p][0]], 1)
                if kind == 1:
                    misc_wait_freed(dve, ("mod", p))
                    for vv in range(2):
                        g = cols[:, 32 + 8 * half:40 + 8 * half]
                        ins = nc.vector.scalar_tensor_tensor(gain1[:, f, vv], mods[:, 1, f, vv], 1.0, g, ALU.add, ALU.mult)
                        if vv == 0:
                            then(ins)
                    ins.then_inc(gain_ready, 1)

            for p in range(4):
                p0_chunk(p)
                if p == 0:
                    dve.wait_ge(rstd_ready, 1)
                    for n, t in enumerate([xt, xt, ct, ct]):
                        nc.vector.tensor_scalar(t[:, n % 2, :], t[:, n % 2, :], rsx[:, n:n + 1], None, ALU.mult)\
                            .then_inc(xn_ready, 1)
                    dve.wait_ge(rope_in, 64)
                    rope_tables(1)
            mod_columns(3)

            def modulate_lo(k):
                for vv, (src, dst) in enumerate(((xhT, hT), (chT, cT))):
                    n = 2 * k + vv
                    misc_wait_freed(dve, (("x", "c")[vv], k))
                    dve.wait_ge(gain_ready, 1 if k < 4 else 2)
                    if n >= 2:
                        dve.wait_ge(h_lo, n - 1)
                    for j in range(2):
                        f = 2 * k + j
                        nc.vector.tensor_scalar(hmod[:, vv, j, :], src[:, f, :], gain1[:, f, vv:vv + 1],
                                                mods[:, 0, f, vv:vv + 1], ALU.mult, ALU.add).then_inc(h_tmp, 1)
                    dve.wait_ge(h_tmp, 2 * n + 2)
                    dve.wait_ge(h_hi, 2 * n + 2)
                    nc.vector.tensor_tensor(dst[1][:, 2 * k:2 * k + 2, :], hmod[:, vv, :, :],
                                            dst[0][:, 2 * k:2 * k + 2, :].bitcast(F32), ALU.subtract).then_inc(h_lo, 1)

            def split_lo(n_wh, s, m):
                dve.wait_ge(wh_done, n_wh)
                nc.vector.tensor_tensor(wl[:, m % SPL, :], raw[:, s % RAW, :], wh[:, m % SPL, :].bitcast(F32), ALU.subtract)\
                    .then_inc(wl_done, 1)

            def mac(j):
                jc, k = divmod(j, KT)
                s = STREAM.index(("A", jc, k))
                dve.wait_ge(raw_full[s % RAW], 16 * (s // RAW + 1))
                if k == 0:
                    dve.wait_ge(p0_sum, 4)
                    if jc >= 2:
                        misc_wait_full(dve, ("ada", jc - 2, 0 if jc < 6 else 1))
                    nc.vector.tensor_scalar(acc[:, jc % 2, :], raw[:, s % RAW, :], cc[:, k, 0:1], None, ALU.mult)\
                        .then_inc(mac_step, 1)
                else:
                    dve.wait_ge(mac_step, j)
                    nc.vector.scalar_tensor_tensor(acc[:, jc % 2, :], raw[:, s % RAW, :], cc[:, k, 0:1], acc[:, jc % 2, :],
                                                   ALU.mult, ALU.add).then_inc(mac_step, 1)

            def rotate(src, dst, t, n):
                c_b = tabC[:, t, :].unsqueeze(1).to_broadcast([P, n, HD])
                s_b = tabS[:, t, :].rearrange("p (j two) -> p j two", two=2)
                s4 = src.rearrange("p (h j two) -> p h j two", h=n, two=2)
                d4 = dst.rearrange("p (h j two) -> p h j two", h=n, two=2)
                for e in range(2):
                    then(nc.vector.tensor_tensor(d4[:, :, :, e], s4[:, :, :, 1 - e],
                                                 s_b[:, :, e].unsqueeze(1).to_broadcast([P, n, HD // 2]), ALU.mult))
                s3 = src.rearrange("p (h d) -> p h d", h=n)
                then(nc.vector.tensor_tensor(s3, s3, c_b, ALU.mult))
                return nc.vector.tensor_tensor(dst, dst, src, ALU.add)

            def cut(t, col):
                return lambda b: t[:, b % 2, col + b // 2 * HC:col + (b // 2 + 1) * HC]

            def post(m):
                if m in ADA_SUM:
                    jc = ADA_SUM[m]
                    if jc < 4:
                        kind, half = divmod(jc, 2)
                        b = misc_wait_full(dve, ("ada", jc, 0))
                        f = slice(8 * half, 8 * half + 8)
                        nc.vector.tensor_tensor(mods2[:, kind, f], b[:, 0:8],
                                                cols[:, 96 + 16 * kind + 8 * half:104 + 16 * kind + 8 * half], ALU.add)\
                            .then_inc(misc_free[MISC_AT["ada", jc, 0][0]], 1)
                        if kind == 1:
                            misc_wait_freed(dve, ("ada", jc, 0))
                            nc.vector.scalar_tensor_tensor(gain2[:, f], mods2[:, 1, f], 1.0,
                                                           cols[:, 48 + 8 * half:56 + 8 * half], ALU.add, ALU.mult)\
                                .then_inc(g_done, 1)
                    else:
                        row, arrived = ((g1row, g1_in), (g2row, g2_in))[(jc - 4) // 2]
                        dve.wait_ge(arrived, 16)
                        for half in range(2):
                            b = misc_wait_full(dve, ("ada", jc, half))
                            col = jc % 2 * NC + half * HC
                            nc.vector.tensor_tensor(row[:, col:col + HC], row[:, col:col + HC], b[:], ALU.add)\
                                .then_inc(misc_free[MISC_AT["ada", jc, half][0]], 1)
                t = m - LAST["K"] - 3
                if 0 <= t < 4:
                    src, dst = kraw[:, t, :], krot[:, t, :]
                    dve.wait_ge(sqk_ready, 4 * (t + 1))
                    s3 = src.rearrange("p (h d) -> p h d", h=NKV)
                    d3 = dst.rearrange("p (h d) -> p h d", h=NKV)
                    if t < TB:
                        then(rotate(src, dst, t, NKV))
                    else:
                        then(nc.vector.tensor_tensor(d3, s3, gq[:, 1, :].unsqueeze(1).to_broadcast([P, NKV, HD]), ALU.mult))
                    if t == 3:
                        dve.wait_ge(rstd_ready, 2)
                        for w in range(4):
                            w3 = krot[:, w, :].rearrange("p (h d) -> p h d", h=NKV)
                            nc.vector.tensor_tensor(w3, w3, rsk[:, 4 * w:4 * w + 4].unsqueeze(2).to_broadcast([P, NKV, HD]),
                                                    ALU.mult).then_inc(kn_ready, 1)
                        rope_tables(0)
                if m in FOUR2:
                    g = FOUR2[m]
                    b = misc_wait_full(dve, ("four2", g))
                    dve.wait_ge(hi_done, HI_AT["f", g])
                    nc.vector.tensor_tensor(yT[1][:, 2 * g:2 * g + 2, :].rearrange("p f t -> p (f t)"), b[:],
                                            yT[0][:, 2 * g:2 * g + 2, :].rearrange("p f t -> p (f t)").bitcast(F32),
                                            ALU.subtract).then_inc(misc_free[MISC_AT["four2", g][0]], 1)
                if m in ROPE_Q:
                    ch, g = ROPE_Q[m]
                    t, half = divmod(g, 2)
                    dve.wait_ge(sqq_ready, 16 * ch + 4 * (g + 1))
                    if ch:
                        misc_wait_full(dve, ("q", (0, 3)))
                    cols_q = slice(half * HC, (half + 1) * HC)
                    rotate(qraw[:, t, cols_q], qrot[:, t, cols_q], t, 4).then_inc(qr_ready, 1)
                if m in SLOTS:
                    u = SLOTS[m]
                    if u < UNITS:
                        h, t = divmod(u, TB)
                        col = 8 * t + h % 8
                        dve.wait_ge(s_done, u + 1)
                        then(nc.vector.tensor_reduce(mx[:, u:u + 1], bank[4][:], AX.X, ALU.max))
                        dve.wait_ge(rstd_ready, 3 + h // 8)
                        nc.vector.tensor_tensor(nb[:, u:u + 1], mx[:, u:u + 1], nqs[:, h // 8, col:col + 1], ALU.mult)\
                            .then_inc(nb_ready, 1)
                    if 1 <= u < UNITS + 1:
                        w = u - 1
                        dve.wait_ge(exp_done, w + 1)
                        then(nc.vector.reciprocal(rinv[:, w:w + 1], rsum[:, w:w + 1]))
                        nc.vector.tensor_scalar(probs[:, w % 2, :], probs[:, w % 2, :], rinv[:, w:w + 1], None, ALU.mult)\
                            .then_inc(pn_ready, 1)
                if m in OL:
                    g = OL[m]
                    dve.wait_ge(pv_done, UNITS)
                    dve.wait_ge(hi_done, HI_AT["o", g])
                    nc.vector.tensor_tensor(oS[1][:, 4 * g:4 * g + 4, :], oT[:, 4 * g:4 * g + 4, :],
                                            oS[0][:, 4 * g:4 * g + 4, :].bitcast(F32), ALU.subtract).then_inc(ol_done, 1)
                for ch in range(2):
                    if m == LAST[f"A{ch}"]:
                        dve.wait_ge(bank_free, 4 * CI["GF1"] + 4)
                        for b in range(4):
                            wait_bank(dve, CI[f"A{ch}"], m, b)
                            part = cut(gateA, ch * NC)(b)
                            nc.vector.scalar_tensor_tensor(part, part, 1.0, bank[b][:], ALU.add, ALU.mult)\
                                .then_inc(bank_free, 1)
                    if m == LAST[f"B{ch}"]:
                        for b in range(4):
                            wait_bank(dve, CI[f"B{ch}"], m, b)
                            part = cut(gateF, ch * NC)(b)
                            nc.vector.scalar_tensor_tensor(part, part, 1.0, bank[b][:], ALU.add, ALU.mult)\
                                .then_inc(bank_free, 1)
                        for b in range(4):
                            dve.wait_ge(bank_free, 4 * CI[f"B{ch}"] + b + 1)
                            part = cut(gateA, ch * NC)(b)
                            nc.vector.tensor_tensor(part, part, cut(gateF, ch * NC)(b), ALU.add).then_inc(mid_done, 1)
                    if m == LAST[f"O{ch}"]:
                        dve.wait_ge(xr_in, 16)
                        for b in range(4):
                            n = 4 * ch + b
                            wait_bank(dve, CI[f"O{ch}"], m, b)
                            col = ch * NC + b // 2 * HC
                            if ch:
                                dve.wait_ge(x1_ready, b + 1)
                            nc.vector.tensor_tensor(scr[:, b, :], bank[b][:], g1row[:, col:col + HC], ALU.mult)\
                                .then_inc(bank_free, 1)
                            dve.wait_ge(bank_free, 4 * CI[f"O{ch}"] + b + 1)
                            part = cut(x1, ch * NC)(b)
                            nc.vector.tensor_tensor(part, part, scr[:, b, :], ALU.add).then_inc(x1_ready, 1)
                if m in MTR:
                    ch, g = MTR[m]
                    b = misc_wait_full(dve, ("m", (ch, g)))
                    dve.wait_ge(hi_done, HI_AT["m", (ch, g)])
                    f = 8 * ch + 2 * g
                    nc.vector.scalar_tensor_tensor(mT[1][:, f:f + 2, :].rearrange("p f t -> p (f t)"), b[:], 0.5,
                                                   mT[0][:, f:f + 2, :].rearrange("p f t -> p (f t)").bitcast(F32),
                                                   ALU.mult, ALU.subtract)\
                        .then_inc(misc_free[MISC_AT["m", (ch, g)][0]], 1)

            def modulate2_lo(g):
                b = misc_wait_full(dve, ("xs", g))
                dve.wait_ge(hi_done, HI_AT["xs", 2 * g + 1])
                if g >= 2:
                    misc_wait_freed(dve, ("xs", g - 2))
                for j in range(2):
                    f = 2 * g + j
                    then(nc.vector.tensor_scalar(hmod2[:, g % 2, j, :], b[:, j * T:(j + 1) * T], gain2[:, f:f + 1],
                                                 mods2[:, 0, f:f + 1], ALU.mult, ALU.add))
                nc.vector.tensor_tensor(h2T[1][:, 2 * g:2 * g + 2, :], hmod2[:, g % 2, :, :],
                                        h2T[0][:, 2 * g:2 * g + 2, :].bitcast(F32), ALU.subtract)\
                    .then_inc(misc_free[MISC_AT["xs", g][0]], 1)

            for m, (name, k) in enumerate(TILES):
                if name == "K":
                    modulate_lo(k)
                split_lo(m + 1, STREAM_AT["M", m], m)
                for j in ADA_AT[m]:
                    mac(j)
                if m >= AHEAD:
                    post(m - AHEAD)

            def lo_1(i, k):
                split_lo(i * KT + (M1 + k + 1), S1 + k, k)

            def relu(i):
                for b in range(4):
                    if b < 3:
                        dve.wait_ge(bank_full, i * 3 + (3 * CI1 + b + 1))
                    else:
                        dve.wait_ge(gemm_done, i * KT + (M1 + KT))
                    if b == 0:
                        if not (isinstance(i, int) and i == 0):
                            dve.wait_ge(hT_full, i * 4)
                    nc.vector.tensor_scalar(hs[:, b % 2, b // 2 * HC:(b // 2 + 1) * HC], bank[b][:], 0.0, None, ALU.max)\
                        .then_inc(bank_free, 1)

            for k in range(KT):
                lo_1(0, k)
                if k < AHEAD:
                    post(M1 - AHEAD + k)
                if k == AHEAD - 1:
                    dve.wait_ge(rstd_ready, 5)
                    for half in range(2):
                        for t in range(TB):
                            nc.vector.tensor_scalar(xs[:, t, half * NC:(half + 1) * NC], x1[:, t, half * NC:(half + 1) * NC],
                                                    rs1[:, t:t + 1], None, ALU.mult).then_inc(xs_ready, 1)
                    dve.wait_ge(g_done, 2)
                    for g in range(XS_NOW):
                        modulate2_lo(g)
                if AHEAD <= k and XS_NOW + k - AHEAD < 8:
                    modulate2_lo(XS_NOW + k - AHEAD)
            with nc.vector.Fori(1, N1) as i:
                for k in range(KT):
                    lo_1(i, k)
                    if k == 1:
                        relu(i - 1)

            def lo_2(g, j):
                if j % 4 == 0:
                    q = j // 4
                    dve.wait_ge(hs_hi, g * 2 + (q + 1))
                    nc.vector.tensor_tensor(hidS[1][:, q, :, :], hid[:, bass.ds(g * 4 + 2 * q, 2), :],
                                            hidS[0][:, q, :, :].bitcast(F32), ALU.subtract).then_inc(hs_lo, 1)
                split_lo(g * 8 + (M2 + j + 1), S1 + j, j)

            for j in range(8):
                lo_2(0, j)
                if j == 1:
                    relu(N1 - 1)
            with nc.vector.Fori(1, N2 // 8) as g:
                for j in range(8):
                    lo_2(g, j)
            for b in range(8):
                n, half, t = b // 4, b // 2 % 2, b % 2
                if b % 4 < 3:
                    dve.wait_ge(bank_full, 3 * (CI1 + N1) + 3 * n + b % 4 + 1)
                else:
                    dve.wait_ge(gemm_done, M2 + N2 - 1 + n)
                col = n * NC + half * HC
                then(nc.vector.tensor_tensor(scr2[:, b, :], bank[b][:], g2row[:, col:col + HC], ALU.mult))
                nc.vector.tensor_tensor(x1[:, t, col:col + HC], x1[:, t, col:col + HC], scr2[:, b, :], ALU.add)\
                    .then_inc(x2_ready, 1)
            dve.wait_ge(rstd_ready, 6)
            dve.wait_ge(fg_in, 16)
            for t in range(TB):
                nc.vector.scalar_tensor_tensor(res[:, t, :], x1[:, t, :], rs2[:, t:t + 1], fgrow[:], ALU.mult, ALU.mult)\
                    .then_inc(res_ready, 1)

        @block.tensor
        def _(pe):
            def misc_take(key):
                b, n = MISC_AT[key]
                if n:
                    pe.wait_ge(misc_free[b], n)
                return bank[b], misc_full[b]

            def products(b, terms, start, stop):
                for j, (a_hi, a_lo, w_hi, w_lo) in enumerate(terms):
                    first, last = start and j == 0, stop and j == len(terms) - 1
                    nc.tensor.matmul(bank[b][:], a_hi, w_hi, start=first, stop=False)
                    nc.tensor.matmul(bank[b][:], a_hi, w_lo, start=False, stop=False)
                    ins = nc.tensor.matmul(bank[b][:], a_lo, w_hi, start=False, stop=last)
                return ins

            def tile_products(a, k, slot, banks, start, stop, free=None):
                for n, b in enumerate(banks):
                    half, t = n // 2, n % 2
                    if free is not None:
                        pe.wait_ge(bank_free, free + n)
                    w = slice(half * HC, (half + 1) * HC)
                    cols_t = slice(t * P, (t + 1) * P)
                    ins = products(b, [(a[0][:, k, cols_t], a[1][:, k, cols_t], wh[:, slot, w], wl[:, slot, w])], start, stop)
                    if n == 3:
                        ins.then_inc(gemm_done, 1)
                    elif stop:
                        ins.then_inc(bank_full, 1)

            pe.wait_ge(ident_in, 16)
            pe.wait_ge(vec_in, 96)
            pe.wait_ge(const_set, 5)
            b, full = misc_take(("vec", 0))
            nc.tensor.transpose(b[:, 0:P], rows[:], ident[:]).then_inc(full, 1)
            pe.wait_ge(cc_ready, 1)

            def token_transposes(key, src, f0):
                b, full = misc_take(key)
                for n in range(4):
                    f, t = f0 + n // 2, n % 2
                    ins = nc.tensor.transpose(b[:, n * P:(n + 1) * P], src[:, t, f * P:(f + 1) * P], ident[:])
                ins.then_inc(full, 1)

            n_mm = 0
            for p in range(4):
                banks = [bank[2 * (p % 2)], bank[2 * (p % 2) + 1]]
                n_tr = 0
                for k in range(KT):
                    if p in (1, 2) and n_tr < 8 and k % 2 == 0:
                        pe.wait_ge(xn_ready, 2 * p)
                        token_transposes((("x", "c")[p - 1], n_tr), (xt, ct)[p - 1], 2 * n_tr)
                        n_tr += 1
                    if k in P0_DVE:
                        continue
                    s = p * KT + k
                    pe.wait_ge(raw_full[s % RAW], 16 * (s // RAW + 1))
                    if k == 0 and p >= 2:
                        pe.wait_ge(modrow_ready, 2 * (p - 1))
                    for half in range(2):
                        ins = nc.tensor.matmul(banks[half][0:2, :], cc[:, k, :], raw[:, s % RAW, half * HC:(half + 1) * HC],
                                               start=(k == 0), stop=False)
                    ins.then_inc(p0_mm, 1)
                pe.wait_ge(acc_step, 2 * len(P0_DVE) * (p + 1))
                for half in range(2):
                    for vv in range(2):
                        ins = nc.tensor.matmul(banks[half][0:2, :], pick[:, vv, :], acc[:, vv, half * HC:(half + 1) * HC],
                                               start=False, stop=(vv == 1))
                ins.then_inc(p0_sum, 1)
                pe.wait_ge(modrow_ready, 2 * (p + 1))
                b, full = misc_take(("mod", p))
                for f in range(8):
                    ins = nc.tensor.transpose(b[:, 2 * f:2 * f + 2], modrow[:, f * P:(f + 1) * P], ident[0:2, 0:2])
                ins.then_inc(full, 1)

            def hook(m):
                if m in ADA_SUM:
                    jc = ADA_SUM[m]
                    pe.wait_ge(mac_step, KT * (jc + 1))
                    if jc < 4:
                        b, full = misc_take(("ada", jc, 0))
                        for f in range(8):
                            ins = nc.tensor.matmul(b[:, f:f + 1], acc[:, jc % 2, f * P:(f + 1) * P], ones[:, 0:1],
                                                   start=True, stop=True)
                        ins.then_inc(full, 1)
                    else:
                        for half in range(2):
                            b, full = misc_take(("ada", jc, half))
                            nc.tensor.matmul(b[:], ones[:], acc[:, jc % 2, half * HC:(half + 1) * HC],
                                             start=True, stop=True).then_inc(full, 1)
                if m in KTR:
                    t = KTR[m]
                    pe.wait_ge(kn_ready, t + 1)
                    b, full = misc_take(("k", t))
                    for h in range(NKV):
                        ins = nc.tensor.transpose(b[:, h * P:(h + 1) * P], krot[:, t, h * HD:(h + 1) * HD], ident[:])
                    ins.then_inc(full, 1)
                if m in FOUR1:
                    d = FOUR1[m]
                    if d == 0:
                        pe.wait_ge(dft_in, 16)
                    b, full = misc_take(("four1", d))
                    for t in range(TB):
                        ins = nc.tensor.matmul(b[:], fin[:, t, d * P:(d + 1) * P], dft_sb[:, t, 0:2 * FG],
                                               start=(t == 0), stop=(t == TB - 1))
                    ins.then_inc(full, 1)
                if m in FOUR2:
                    g = FOUR2[m]
                    if g == 0:
                        for d in range(8):
                            misc_wait_freed(pe, ("four1", d))
                    b, full = misc_take(("four2", g))
                    for o in range(2):
                        for e in range(2):
                            for part, tab in ((0, 0), (1, 2 * FG)):
                                ins = nc.tensor.matmul(b[:, o * T:(o + 1) * T], dft_sb[:, e, tab + o * P:tab + (o + 1) * P],
                                                       ab[:, 2 * g + e, part * T:(part + 1) * T],
                                                       start=(e == 0 and part == 0), stop=(e == 1 and part == 1))
                    ins.then_inc(full, 1)
                if m in QTR:
                    ch, g = QTR[m]
                    t, half = divmod(g, 2)
                    pe.wait_ge(qr_ready, 4 * ch + g + 1)
                    b, full = misc_take(("q", (ch, g)))
                    for h in range(4):
                        col = half * HC + h * HD
                        ins = nc.tensor.transpose(b[:, h * P:(h + 1) * P], qrot[:, t, col:col + HD], ident[:])
                    ins.then_inc(full, 1)
                if m in SLOTS:
                    u = SLOTS[m]
                    if u == 0:
                        for t in range(4):
                            misc_wait_freed(pe, ("k", t))
                        pe.wait_ge(bank_free, 4 * CI["V"] + 4)
                        for bb in (6, 7):
                            pe.wait_ge(misc_free[bb], max(n + 1 for key, (x_, n) in MISC_AT.items()
                                                          if x_ == bb and MISC.index(key) < _busy_from))
                    if u < UNITS:
                        h, t = divmod(u, TB)
                        if h % 8 == 0 and t == 0:
                            for g in range(4):
                                misc_wait_freed(pe, ("q", (h // 8, g)))
                        if u:
                            pe.wait_ge(exp_done, u)
                        nc.tensor.matmul(bank[4][:], qT[:, h, t * P:(t + 1) * P], kT[:, h // QPK, :],
                                         start=True, stop=True).then_inc(s_done, 1)
                    if 2 <= u < UNITS + 2:
                        w = u - 2
                        pe.wait_ge(pn_ready, w + 1)
                        if w:
                            pe.wait_ge(pt_ready, w)
                        for kb in range(4):
                            ins = nc.tensor.transpose(bank[6][:, kb * P:(kb + 1) * P], probs[:, w % 2, kb * P:(kb + 1) * P],
                                                      ident[:])
                        ins.then_inc(pt_full, 1)
                    if 3 <= u:
                        w = u - 3
                        h, t = divmod(w, TB)
                        pe.wait_ge(pt_ready, w + 1)
                        if w:
                            pe.wait_ge(o_ready, w)
                        for kb in range(4):
                            ins = nc.tensor.matmul(bank[7][:, 0:P], v[:, kb, h // QPK * HD:(h // QPK + 1) * HD],
                                                   probsT[:, w % 2, kb, :], start=(kb == 0), stop=(kb == 3))
                        ins.then_inc(pv_done, 1)
                if m in MTR:
                    ch, g = MTR[m]
                    if ch == 0 and g == 0:
                        pe.wait_ge(o_ready, UNITS)
                    pe.wait_ge(mid_done, 4 * (ch + 1))
                    token_transposes(("m", (ch, g)), gateA, 8 * ch + 2 * g)

            for m, (name, k) in enumerate(TILES):
                last = m == LAST[name]
                if name == "K":
                    pe.wait_ge(h_lo, 2 * (k + 1))
                pe.wait_ge(wl_done, m + 1)
                if name in "KV":
                    for t in range(4):
                        if k == 0:
                            if name == "K":
                                pe.wait_ge(modrow_ready, 8)
                            else:
                                pe.wait_ge(bank_free, 4 * CI["K"] + t + 1)
                        a = hT if t < TB else cT
                        cols_t = slice(t % 2 * P, (t % 2 + 1) * P)
                        ins = products(t, [(a[0][:, 2 * k + j, cols_t], a[1][:, 2 * k + j, cols_t],
                                            wh[:, m % SPL, j * HC:(j + 1) * HC], wl[:, m % SPL, j * HC:(j + 1) * HC])
                                           for j in range(2)], k == 0, last)
                        if t == 3:
                            ins.then_inc(gemm_done, 1)
                        elif last:
                            ins.then_inc(bank_full, 1)
                else:
                    a = {"A": oS, "B": yT, "O": mT}.get(name[0], hT)
                    if name[0] == "A" and k % 4 == 0:
                        pe.wait_ge(ol_done, k // 4 + 1)
                    if name == "B0" and k == 0:
                        for g in range(4):
                            misc_wait_freed(pe, ("four2", g))
                    if name[0] == "O" and k % 2 == 0 and name == "O0":
                        misc_wait_freed(pe, ("m", divmod(k // 2, 4)))
                    tile_products(a, k, m % SPL, range(4), k == 0, last, 4 * CI[name] - 3 if k == 0 else None)
                hook(m)

            def xs_transposes(g):
                pe.wait_ge(xs_ready, 2 if g < 4 else 4)
                token_transposes(("xs", g), xs, 2 * g)

            for g in range(XS_NOW):
                xs_transposes(g)

            def first_product(i, k):
                pe.wait_ge(wl_done, i * KT + (M1 + k + 1))
                if isinstance(i, int) and i == 0 and k % 2 == 0:
                    misc_wait_freed(pe, ("xs", k // 2))
                tile_products(h2T, k, k % SPL, range(4), k == 0, k == KT - 1,
                              i * 4 + (4 * CI1 - 3) if k == 0 else None)

            def hidden_transposes(i, g):
                if g == 0:
                    pe.wait_ge(bank_free, i * 4 + 4 * (CI1 + 1))
                if isinstance(i, int) and i == 0:
                    if g in (1, 2, 3):
                        pe.wait_ge(misc_free[4 + g], _uses[4 + g])
                else:
                    pe.wait_ge(hid_ready, i * 4 + (g - 3))
                for n in range(4):
                    f, t = 2 * g + n // 2, n % 2
                    ins = nc.tensor.transpose(bank[4 + g][:, n * P:(n + 1) * P], hs[:, t, f * P:(f + 1) * P], ident[:])
                ins.then_inc(hT_full, 1)

            for k in range(KT):
                first_product(0, k)
                if XS_NOW + k < 8:
                    xs_transposes(XS_NOW + k)
            for k in range(KT):
                first_product(1, k)
                if 1 <= k < 5:
                    hidden_transposes(0, k - 1)
            with nc.tensor.Fori(2, N1) as i:
                for k in range(KT):
                    first_product(i, k)
                    if 1 <= k < 5:
                        hidden_transposes(i - 1, k - 1)
            for g in range(4):
                hidden_transposes(N1 - 1, g)

            def second_product(g, j, start, stop):
                if j % 4 == 0:
                    pe.wait_ge(hs_lo, g * 2 + (j // 4 + 1))
                pe.wait_ge(wl_done, g * 8 + (M2 + j + 1))
                n = j % 2
                if start and j == 0:
                    pe.wait_ge(bank_free, 4 * (CI1 + N1))
                if start and j == 1:
                    pe.wait_ge(hid_ready, 4 * N1)
                q, e = divmod(j // 2, 2)
                tile_products([hidS[0][:, q, :, :], hidS[1][:, q, :, :]], e, j % SPL, range(4 * n, 4 * n + 4),
                              start and j < 2, stop and j >= 6)

            for j in range(8):
                second_product(0, j, True, False)
            with nc.tensor.Fori(1, N2 // 8 - 1) as g:
                for j in range(8):
                    second_product(g, j, False, False)
            for j in range(8):
                second_product(N2 // 8 - 1, j, False, True)


def constants():
    n = np.arange(T)
    angle = 2 * np.pi * np.outer(n, n) % (2 * np.pi * T) / T
    cos, sin = np.cos(angle) / 16.0, np.sin(angle) / 16.0
    pairs = HD // 4
    inv = 1.0 / (10000.0 ** (np.arange(pairs, dtype=np.float32) / np.float32(pairs)))
    inv = inv.astype(np.float32)
    row = (n // 64).astype(np.float32)[:, None] * inv
    col = (n % 64).astype(np.float32)[:, None] * inv
    ang = np.concatenate([row, col], axis=1).astype(np.float64)
    c, s = np.cos(ang), np.sin(ang)
    return {
        "identity": np.eye(P, dtype=np.float32),
        "dft": np.concatenate([cos, sin, -sin], axis=1).astype(np.float32),
        "rope_c": np.repeat(c, 2, axis=1).astype(np.float32),
        "rope_s": np.stack([-s, s], axis=-1).reshape(T, HD).astype(np.float32),
    }


INPUTS = ["x", "c", "ctx", "c_ctx", "w_ada", "b_ada", "norm1_g", "w_in", "q_norm_g", "k_norm_g", "w_attn_o",
          "w_fourier", "w_out", "norm2_g", "w1", "w2", "final_norm_g"]


def kernel(**inputs):
    import concourse.bacc as bacc
    from concourse.bass_utils import run_bass_kernel_spmd

    nc = bacc.Bacc("TRN2", target_bir_lowering=False, num_devices=1, dynamic_dma_scratch_size=1024)
    arrays, args = {}, []
    for name in INPUTS:
        a = np.ascontiguousarray(inputs[name])
        if a.shape[0] == 1 and a.ndim > 1:
            a = a[0]
        arrays[f"in_{name}"] = a
    arrays |= {f"in_{name}": a for name, a in constants().items()}
    for name, a in arrays.items():
        args.append(nc.dram_tensor(name, a.shape, mybir.dt.from_np(a.dtype), kind="ExternalInput").ap())
    out = nc.dram_tensor("out_0", (T, D), F32, kind="ExternalOutput").ap()
    block_program(nc, *args, out)
    got = run_bass_kernel_spmd(nc, [arrays], core_ids=[0])
    return got.results[0]["out_0"].reshape(1, T, D)
```

```python
from contextlib import ExitStack

import numpy as np

import concourse.bass as bass
from concourse import mybir

F32 = mybir.dt.float32
F32R = mybir.dt.float32r
ALU = mybir.AluOpType
ACT = mybir.ActivationFunctionType
AX = mybir.AxisListType

P = 128
D = 2048
T = 256
TB = T // P
KT = D // P
HD = 128
NH = 16
NKV = 4
QPK = NH // NKV
DFF = 4 * D
FW = 1024
FG = 256
NC = 1024
HC = 512
EPS = 1e-6
SCALE = HD ** -0.5
K0, V0, FO0, GA0, GF0 = 2048, 2560, 3072, 4096, 6144

RAW = 8
SPL = 4
MORE = 2
AHEAD = 2
AHEAD_MODS = 4

CHUNKS = [("K", 8), ("V", 8), ("F", 16), ("Q0", 16), ("Q1", 16), ("GA0", 16), ("GA1", 16),
          ("GF0", 16), ("GF1", 16), ("A0", 16), ("B0", 8), ("A1", 16), ("B1", 8), ("O0", 16), ("O1", 16)]
CI = {name: i for i, (name, _) in enumerate(CHUNKS)}
MODS = [kind + str(q) for q in range(4) for kind in "SC"]
TWO_BLOCKS = ["K", "V"] + MODS
MOD_BANK = {"S": 4, "C": 7}
K_AMONG = {("S1", 7), ("C1", 4), ("S2", 7), ("C2", 4)}
TILES, _k = [], 0
for _name in MODS:
    for _n in range(KT // 2):
        TILES.append((_name, _n))
        if (_name, _n) in K_AMONG:
            TILES.append(("K", _k))
            _k += 1
MODS_END = len(TILES)
for _name, _n in CHUNKS:
    TILES += [(_name, k) for k in range(_k if _name == "K" else 0, _n)]
LAST = {name: m for m, (name, _) in enumerate(TILES)}
FIRST = {name: TILES.index((name, 0)) for name in LAST}
M1 = len(TILES)
N1 = DFF // NC
M2 = M1 + N1 * KT
N2 = DFF // P * (D // NC)
CI1 = len(CHUNKS)

MORE_END = MODS_END - 6
SLOT_OF = [m % (SPL + MORE) if m < MORE_END else m % SPL for m in range(M1)]
BEFORE = [max((j for j in range(m) if SLOT_OF[j] == SLOT_OF[m]), default=None) for m in range(M1)]
assert M1 % SPL == 0
POSTS, _at = {}, 0
for _m in range(M1 - AHEAD):
    _at = max(_at, min(_m + AHEAD_MODS, MODS_END + 1) if _m < MODS_END else _m + AHEAD)
    if _m in (LAST[f"{g}{h}"] for g in ("GA", "GF") for h in range(2)):
        POSTS.setdefault(_at - 1, []).append(_m)
    else:
        POSTS.setdefault(_at, []).append(_m)

ADA_COLS = [6, 7, 8, 9, 4, 5, 10, 11]
STREAM = []
ADA_AT = {}
ADA_END = {}
_units, _n = 0.0, 0
for _m, (_name, _k) in enumerate(TILES):
    STREAM.append(("M", _m, 0))
    _units += 0.0 if _m < MODS_END + 2 else 2.0 if _name in "KV" else 1.0
    ADA_AT[_m] = []
    while _n < 128 and _n < _units * 0.62:
        ADA_AT[_m].append(_n)
        STREAM.append(("A", _n // KT, _n % KT))
        if _n % KT == KT - 1:
            ADA_END[_m] = _n // KT
        _n += 1
assert _n == 128
S1 = len(STREAM)
STREAM_AT = {("M", m): i for i, (kind, m, _) in enumerate(STREAM) if kind == "M"}

K_TILES = dict(CHUNKS)["K"]
K_AT = [TILES.index(("K", k)) for k in range(K_TILES)]
MODULATE = {K_AT[k] - 3: k for k in range(6)} | {K_AT[k]: k for k in (6, 7)}
X_IN = {n: n for n in range(4)}
SQX = {4 + 2 * n: n for n in range(4)}
XN = {11 + n: n for n in range(4)}
TAB_K = 44
MOD_COLS = {LAST[name] + (3 if name != MODS[-1] else 1): p for p, name in enumerate(MODS)}
MOD_ADD = {LAST[name] + 5: p for p, name in enumerate(MODS[:-1])}
XTR = {14 + 2 * n: (("x", "c")[n % 2], n // 2) for n in range(16)}
FOUR1 = {FIRST["Q0"] + 1 + d: d for d in range(8)}
FOUR2 = {FIRST["Q0"] + 9 + g: g for g in range(4)}
KTR = {FIRST["V"] + 6 + t: t for t in range(4)}
SQ_Q = {FIRST["Q0"] + 16 + g: (0, g) for g in range(4)} | {FIRST["Q1"] + 17 + 2 * g: (1, g) for g in range(4)}
ROPE_Q = {FIRST["Q0"] + 17 + g: (0, g) for g in range(4)} | {FIRST["Q1"] + 19 + 2 * g: (1, g) for g in range(4)}
QTR = {FIRST["Q0"] + 19 + g: (0, g) for g in range(4)} | {FIRST["Q1"] + 21 + 2 * g: (1, g) for g in range(4)}
UNITS = NH * TB
SLOT0 = FIRST["Q1"] + 8
SLOTS = {SLOT0 + 2 * u: u for u in range(UNITS + 3)}
OH = {SLOT0 + 2 * UNITS + 1 + g: g for g in range(4)}
OL = {SLOT0 + 2 * (UNITS + 2) + g: g for g in range(4)}
MTR = {FIRST["B0"] + 10 + g: (0, g) for g in range(4)} | {FIRST["O0"] + 1 + g: (1, g) for g in range(4)}
ROWS_FIRST = (0, 2, 1, 3)
LAST_BANKS = (0, 2, 4, 6, 1, 3, 5, 7)
POOL_ADDS = (1, 3, 5)
XS_NOW = 3
G1_LOAD, G2_LOAD, X_LOAD = FIRST["Q0"] + 24, FIRST["A0"] + 4, FIRST["A1"] + 20
ADA_SUM = {m + 1: jc for m, jc in ADA_END.items() if jc < 6}
GATE2 = [("ada", jc, half) for jc in (6, 7) for half in range(2)]

MISC = [("vec", 0)]
for _m in range(M1):
    if _m in MOD_COLS:
        MISC.append(("mod", MOD_COLS[_m]))
    if _m in XTR:
        MISC.append(XTR[_m])
    if _m in ADA_SUM:
        MISC += [("ada", ADA_SUM[_m], h) for h in range(1 if ADA_SUM[_m] < 4 else 2)]
    if _m in KTR:
        MISC.append(("k", KTR[_m]))
    if _m in FOUR1:
        MISC.append(("four1", FOUR1[_m]))
    if _m in FOUR2:
        MISC.append(("four2", FOUR2[_m]))
    if _m in QTR:
        MISC.append(("q", QTR[_m]))
    if _m in MTR:
        MISC.append(("m", MTR[_m]))
MISC += GATE2 + [("xs", g) for g in range(8)]
MISC_AT, _uses = {}, {4: 0, 5: 0, 6: 0, 7: 0}
_busy_from = next(i for i, k in enumerate(MISC) if k == ("q", (0, 3))) + 1
_busy_to = next(i for i, k in enumerate(MISC) if k == ("m", (0, 0)))
_turn = 0
for _i, _key in enumerate(MISC):
    if _key[0] in ("vec", "mod", "x", "c"):
        _b = (5, 6)[_i % 2]
    elif _busy_from <= _i < _busy_to:
        _b = 5
    else:
        _b = (5, 6, 7)[_turn % 3]
        _turn += 1
    MISC_AT[_key] = (_b, _uses[_b])
    _uses[_b] += 1

HI = [("f", g) for g in range(4)] + [("o", g) for g in range(4)]
HI += [("m", k) for k in MTR.values()] + [("xs", k) for k in range(KT)]
HI_AT = {key: i + 1 for i, key in enumerate(HI)}


def block_program(nc, x, c, ctx_, c_ctx, w_ada, b_ada, norm1_g, w_in, q_norm_g, k_norm_g,
                  w_attn_o, w_fourier, w_out, norm2_g, w1, w2, final_norm_g,
                  identity, dft, rope_c, rope_s, out):
    with ExitStack() as stack:
        base = (nc.sbuf_base + 63) // 64 * 64
        where = {}
        at = base
        for region, size in [("raw", RAW * NC * 4 // 1024), ("wh", 16), ("wl", 16), ("acc", 8), ("h", 32), ("x", 16), ("c", 32),
                             ("q", 16), ("kv", 16), ("f", 16), ("p", 8), ("g1", 8)]:
            where[region] = at
            at += size * 1024
        small = [at]

        def place(name, shape, dt, region, skip=0):
            return nc.alloc_sbuf_tensor_at(name, shape, dt, offset=where[region] + skip)

        def little(name, shape, dt=F32):
            t = nc.alloc_sbuf_tensor_at(name, shape, dt, offset=small[0])
            n = 4
            for d in shape[1:]:
                n *= d
            small[0] += (n + 31) // 32 * 32
            return t

        raw = place("raw", [P, RAW, NC], F32, "raw")
        wh = place("wh", [P, SPL, NC], F32R, "wh")
        wl = place("wl", [P, SPL, NC], F32R, "wl")
        wh_more = [place(f"wh_more{i}", [P, NC], F32R, "h", i * 16384 + 12288) for i in range(MORE)]
        wl_more = [place(f"wl_more{i}", [P, NC], F32R, "c", i * 16384 + 12288) for i in range(MORE)]
        acc = place("acc", [P, 2, NC], F32, "acc")
        rows = place("rows", [P, P], F32, "acc")
        pair_sum = place("pair_sum", [4, 2], F32, "acc", 512)
        cc4 = place("cc4", [P, 4 * KT + P], F32R, "acc", 1024)
        hT = [place(f"hT{i}", [P, KT, T], F32R, "h", i * 16384) for i in range(2)]
        cT = [place(f"cT{i}", [P, KT, T], F32R, "c", i * 16384) for i in range(2)]
        oS = [place("oS0", [P, KT, T], F32R, "q"), place("oS1", [P, KT, T], F32R, "kv")]
        mT = [place(f"mT{i}", [P, KT, T], F32R, "h", i * 16384) for i in range(2)]
        h2T = [place(f"h2T{i}", [P, KT, T], F32R, "h", i * 16384) for i in range(2)]
        yT = [place(f"yT{i}", [P, FW // P, T], F32R, "f", i * 8192) for i in range(2)]
        hidS = [place(f"hidS{i}", [P, 2, 2, T], F32R, "f", 8192 + i * 4096) for i in range(2)]
        xt = place("xt", [P, TB, D], F32, "x")
        ct = place("ct", [P, TB, D], F32, "kv")
        junk_x = place("junk_x", [P, D], F32, "h")
        xhT = place("xhT", [P, KT, T], F32, "q")
        chT = place("chT", [P, KT, T], F32, "f")
        modrow = place("modrow", [4, 2, HC], F32, "p")
        hmod = place("hmod", [P, 2, 2, T], F32, "p", 4096)
        kraw = place("kraw", [P, 4, HC], F32, "x")
        krot = place("krot", [P, 4, HC], F32, "x", 8192)
        kT = place("kT", [P, NKV, 2 * T], F32, "kv")
        v = place("v", [P, 2 * TB, HC], F32, "kv", 8192)
        fin = place("fin", [P, TB, FW], F32, "f")
        ab = place("ab", [P, FW // P, 2 * T], F32, "x")
        qraw = place("qraw", [P, TB, NC], F32, "x")
        qrot = place("qrot", [P, TB, NC], F32, "x", 8192)
        qT = place("qT", [P, NH, T], F32, "q")
        probs = place("probs", [P, 2, 2 * T], F32, "p")
        probsT = place("probsT", [P, 2, 4, P], F32, "p", 4096)
        oT = place("oT", [P, NH, T], F32, "c")
        gateA = place("gateA", [P, TB, D], F32, "x")
        gateF = place("gateF", [P, TB, D], F32, "c", 16384)
        x1 = place("x1", [P, TB, D], F32, "kv")
        scr = place("scr", [P, 4, HC], F32, "f")
        junk_1 = place("junk_1", [P, 4, HC], F32, "f", 8192)
        xs = place("xs", [P, TB, D], F32, "x")
        hs = place("hs", [P, TB, NC], F32, "f")
        hmod2 = place("hmod2", [P, 2, 2, T], F32, "f", 8192)
        hid = place("hid", [P, DFF // P, T], F32, "x")
        g1row = place("g1row", [P, D], F32, "g1")
        dft_sb = place("dft_sb", [P, TB, 3 * FG], F32, "g1")
        ropeC = place("ropeC", [P, TB, HD], F32, "g1", TB * 3 * FG * 4)
        ropeS = place("ropeS", [P, TB, HD], F32, "g1", TB * (3 * FG + HD) * 4)
        g2row = place("g2row", [P, D], F32, "p")
        fgrow = place("fgrow", [P, D], F32, "g1")
        scr2 = place("scr2", [P, 8, HC], F32, "h")
        junk_2 = place("junk_2", [P, 8, HC], F32, "h", 16384)
        res = place("res", [P, TB, D], F32, "x")
        ident = little("ident", [P, P])
        ones = little("ones", [P, P])
        cols = little("cols", [P, P])
        th = little("th", [P, 2, KT])
        cc = little("cc", [P, KT, 2])
        mods = little("mods", [P, 2, KT, 2])
        gain1 = little("gain1", [P, KT, 2])
        mods2 = little("mods2", [P, 2, KT])
        gain2 = little("gain2", [P, KT])
        tabC = little("tabC", [P, TB, HD])
        tabS = little("tabS", [P, TB, HD])
        gq = little("gq", [P, 2, HD])
        ssx = little("ssx", [P, 4])
        ssk = little("ssk", [P, 16])
        ssq = little("ssq", [P, 2, 16])
        ss1 = little("ss1", [P, TB, 4])
        ss2 = little("ss2", [P, TB, 4])
        msum = little("msum", [P, 16])
        msum2 = little("msum2", [P, 4])
        half_neg = little("half_neg", [P, 16])
        rsx = little("rsx", [P, 4])
        rsk = little("rsk", [P, 16])
        rsq = little("rsq", [P, 2, 16])
        qs = little("qs", [P, 2, 16])
        nqs = little("nqs", [P, 2, 16])
        rs1 = little("rs1", [P, TB])
        rs2 = little("rs2", [P, TB])
        mx = little("mx", [P, UNITS])
        nb = little("nb", [P, UNITS])
        rsum = little("rsum", [P, UNITS])
        rinv = little("rinv", [P, UNITS])
        assert small[0] <= nc.sbuf_usable_end, (small[0], nc.sbuf_usable_end)

        bank = [stack.enter_context(nc.psum_tensor(f"bank{i}", [P, HC], F32)) for i in range(8)]

        def hi_slot(m):
            return wh[:, SLOT_OF[m], :] if SLOT_OF[m] < SPL else wh_more[SLOT_OF[m] - SPL][:]

        def lo_slot(m):
            return wl[:, SLOT_OF[m], :] if SLOT_OF[m] < SPL else wl_more[SLOT_OF[m] - SPL][:]

        def wait_x2(eng, i):
            n = sum(j <= i for j in POOL_ADDS)
            if i in POOL_ADDS:
                eng.wait_ge(x2_pool, n)
            else:
                eng.wait_ge(x2_ready, i + 1 - n)

        def last_part(t_all, b):
            n, half, t = b // 4, b // 2 % 2, b % 2
            return t_all[:, t, n * NC + half * HC:n * NC + (half + 1) * HC]

        def sem(name):
            return stack.enter_context(nc.semaphore(name))

        vec_in = sem("vec_in")
        tokens_in = [sem(f"tokens_in{n}") for n in range(4)]
        ident_in = sem("ident_in")
        dft_in = sem("dft_in")
        rope_in = sem("rope_in")
        raw_full = [sem(f"raw_full{i}") for i in range(RAW)]
        g1_in = sem("g1_in")
        g2_in = sem("g2_in")
        xr_in = sem("xr_in")
        fg_in = sem("fg_in")
        stored = sem("stored")
        const_set = sem("const_set")
        pool_step = sem("pool_step")
        dve_step = sem("dve_step")
        tanh_ready = sem("tanh_ready")
        cc_ready = sem("cc_ready")
        cc4_hi = sem("cc4_hi")
        cc4_ready = sem("cc4_ready")
        modrow_ready = sem("modrow_ready")
        sqx_ready = sem("sqx_ready")
        rstd_ready = sem("rstd_ready")
        xn_ready = sem("xn_ready")
        gain_ready = sem("gain_ready")
        h_hi = sem("h_hi")
        h_tmp = sem("h_tmp")
        h_lo = sem("h_lo")
        wh_done = sem("wh_done")
        wl_done = sem("wl_done")
        gemm_done = sem("gemm_done")
        bank_full = sem("bank_full")
        bank_free = sem("bank_free")
        misc_full = {b: sem(f"misc_full{b}") for b in (5, 6, 7)}
        misc_free = {b: sem(f"misc_free{b}") for b in (5, 6, 7)}
        mac_step = sem("mac_step")
        g_done = sem("g_done")
        sqk_ready = sem("sqk_ready")
        sqq_ready = sem("sqq_ready")
        kn_ready = sem("kn_ready")
        qr_ready = sem("qr_ready")
        hi_done = sem("hi_done")
        s_done = sem("s_done")
        nb_ready = sem("nb_ready")
        exp_done = sem("exp_done")
        pn_ready = sem("pn_ready")
        pt_full = sem("pt_full")
        pt_ready = sem("pt_ready")
        pv_done = sem("pv_done")
        o_ready = sem("o_ready")
        ol_done = sem("ol_done")
        mid_done = sem("mid_done")
        x1_ready = sem("x1_ready")
        sq1_ready = sem("sq1_ready")
        xs_ready = sem("xs_ready")
        hT_full = sem("hT_full")
        hid_ready = sem("hid_ready")
        hs_hi = sem("hs_hi")
        hs_lo = sem("hs_lo")
        z_full = sem("z_full")
        gz_ready = sem("gz_ready")
        x2_ready = sem("x2_ready")
        x2_pool = sem("x2_pool")
        sq2_ready = sem("sq2_ready")
        res_ready = sem("res_ready")

        block = stack.enter_context(nc.Block())

        def misc_wait_full(eng, key):
            b, n = MISC_AT[key]
            eng.wait_ge(misc_full[b], n + 1)
            return bank[b]

        def misc_wait_freed(eng, key):
            b, n = MISC_AT[key]
            eng.wait_ge(misc_free[b], n + 1)

        def wait_bank(eng, ci, last, b):
            if b < 3:
                eng.wait_ge(bank_full, 3 * ci + b + 1)
            else:
                eng.wait_ge(gemm_done, last + 1)

        @block.sync
        def _(sp):
            def slot_free(s):
                if s < RAW:
                    return
                kind, a, k = STREAM[s - RAW]
                if kind == "M":
                    sp.wait_ge(wl_done, a + 1)
                else:
                    sp.wait_ge(mac_step, a * KT + k + 1)

            def tile_source(m):
                name, k = TILES[m]
                r = slice(k * P, (k + 1) * P)
                if name in TWO_BLOCKS:
                    w, col = {"K": (w_in, K0), "V": (w_in, V0), "S": (w_ada, 0), "C": (w_ada, D)}[name[0]]
                    if name in MODS:
                        col += int(name[1]) * HC
                    return w[2 * k * P:2 * (k + 1) * P, col:col + HC].rearrange("(t p) n -> p t n", p=P)
                col0 = {"F": FO0, "Q0": 0, "Q1": NC, "GA0": GA0, "GA1": GA0 + NC, "GF0": GF0, "GF1": GF0 + NC}
                if name in col0:
                    return w_in[r, col0[name]:col0[name] + NC]
                n = int(name[1])
                return {"A": w_attn_o, "B": w_fourier, "O": w_out}[name[0]][r, n * NC:(n + 1) * NC]

            for s, (kind, a, k) in enumerate(STREAM):
                if kind == "M" and a == G1_LOAD:
                    b, n = MISC_AT["four2", 3]
                    sp.wait_ge(misc_full[b], n + 1)
                    sp.dma_start(g1row[:], b_ada[2 * D:3 * D].partition_broadcast(P)).then_inc(g1_in, 16)
                if kind == "M" and a == G2_LOAD:
                    sp.wait_ge(pv_done, UNITS)
                    sp.dma_start(g2row[:], b_ada[5 * D:6 * D].partition_broadcast(P)).then_inc(g2_in, 16)
                if kind == "M" and a == X_LOAD:
                    sp.wait_ge(gemm_done, LAST["A1"] + 1)
                    sp.dma_start(x1[:], x.rearrange("(b p) n -> p b n", p=P)).then_inc(xr_in, 16)
                slot_free(s)
                if s == 3:
                    sp.wait_ge(vec_in, 96)
                if kind == "M":
                    src = tile_source(a)
                else:
                    src = w_ada[k * P:(k + 1) * P, ADA_COLS[a] * NC:(ADA_COLS[a] + 1) * NC]
                dst = raw[:, s % RAW, :]
                if kind == "M" and TILES[a][0] in TWO_BLOCKS:
                    dst = dst.rearrange("p (t n) -> p t n", t=2)
                sp.dma_start(dst, src).then_inc(raw_full[s % RAW], 16)

            def load_w1(i, k):
                s = S1 + k
                if isinstance(i, int) and i == 0 and k < RAW:
                    slot_free(s)
                else:
                    sp.wait_ge(wl_done, i * KT + (M1 + k - RAW + 1))
                sp.dma_start(raw[:, s % RAW, :], w1[k * P:(k + 1) * P, bass.ts(i, NC)])\
                    .then_inc(raw_full[s % RAW], 16)

            for k in range(KT):
                load_w1(0, k)
            with nc.sync.Fori(1, N1) as i:
                for k in range(KT):
                    load_w1(i, k)
            with nc.sync.Fori(0, N2 // 8) as g:
                for j in range(8):
                    sp.wait_ge(wl_done, g * 8 + (M2 + j - RAW + 1))
                    sp.dma_start(raw[:, (S1 + j) % RAW, :],
                                 w2[bass.ds(g * 512 + (j // 2) * P, P), (j % 2) * NC:(j % 2 + 1) * NC])\
                        .then_inc(raw_full[(S1 + j) % RAW], 16)
            sp.wait_ge(x1_ready, 8)
            sp.dma_start(fgrow[:], final_norm_g.partition_broadcast(P)).then_inc(fg_in, 16)
            for b in range(TB):
                for half in range(2):
                    part = slice(half * NC, (half + 1) * NC)
                    sp.wait_ge(res_ready, 2 * b + half + 1)
                    sp.dma_start(out[b * P:(b + 1) * P, part], res[:, b, part]).then_inc(stored, 16)
            sp.wait_ge(stored, 16 * 2 * TB)

        @block.gpsimd
        def _(pool):
            nc.gpsimd.memset(ones[:], 1.0).then_inc(const_set, 1)
            nc.gpsimd.memset(cc4[:, 4 * KT:].bitcast(F32), 0.0).then_inc(const_set, 1)
            nc.gpsimd.memset(half_neg[:], -0.5).then_inc(const_set, 1)
            pool.wait_ge(const_set, 3)
            steps = [0]

            def then(ins):
                steps[0] += 1
                ins.then_inc(pool_step, 1)
                pool.wait_ge(pool_step, steps[0])

            def rstd(result, total, mean, width, n):
                then(nc.gpsimd.tensor_scalar(mean, total, 1.0 / width, EPS, ALU.mult, ALU.add))
                return nc.gpsimd.tensor_tensor(result, mean, half_neg[:, 0:n], ALU.pow)

            pool.wait_ge(sqx_ready, 4)
            rstd(rsx[:], ssx[:], msum[:, 0:4], D, 4).then_inc(rstd_ready, 1)
            for k in range(K_TILES):
                for vv, src in enumerate((xhT, chT)):
                    n = 2 * k + vv
                    misc_wait_freed(pool, (("x", "c")[vv], k))
                    pool.wait_ge(gain_ready, k // 2 + 1)
                    if n >= 2:
                        pool.wait_ge(h_lo, n - 1)
                    for j in range(2):
                        f = 2 * k + j
                        nc.gpsimd.tensor_scalar(hmod[:, vv, j, :], src[:, f, :], gain1[:, f, vv:vv + 1],
                                                mods[:, 0, f, vv:vv + 1], ALU.mult, ALU.add).then_inc(h_tmp, 1)
            pool.wait_ge(sqk_ready, 16)
            pool.wait_ge(rstd_ready, 1)
            rstd(rsk[:], ssk[:], msum[:], HD, 16).then_inc(rstd_ready, 1)
            for ch in range(2):
                pool.wait_ge(sqq_ready, 16 * (ch + 1))
                pool.wait_ge(rstd_ready, 2 + ch)
                then(rstd(rsq[:, ch, :], ssq[:, ch, :], msum[:], HD, 16))
                then(nc.gpsimd.tensor_scalar(qs[:, ch, :], rsq[:, ch, :], SCALE, None, ALU.mult))
                nc.gpsimd.tensor_scalar(nqs[:, ch, :], qs[:, ch, :], -1.0, None, ALU.mult).then_inc(rstd_ready, 1)
            for parts, result, seen, before, n in ((ss1, rs1, sq1_ready, (6, 8), 4), (ss2, rs2, sq2_ready, (4, 8), 6)):
                for t in range(TB):
                    for i in (POOL_ADDS if parts is ss2 else ()):
                        if i // 4 == t:
                            pool.wait_ge(gz_ready, POOL_ADDS.index(i) + 1)
                            b = LAST_BANKS[i]
                            nc.gpsimd.tensor_tensor(last_part(x1, b), last_part(x1, b), scr2[:, b, :], ALU.add)\
                                .then_inc(x2_pool, 1)
                    pool.wait_ge(seen, before[t])
                    pool.wait_ge(rstd_ready, n + t)
                    then(nc.gpsimd.tensor_tensor(parts[:, t, 0:2], parts[:, t, 0:2], parts[:, t, 2:4], ALU.add))
                    then(nc.gpsimd.tensor_tensor(msum2[:, 0:1], parts[:, t, 0:1], parts[:, t, 1:2], ALU.add))
                    rstd(result[:, t:t + 1], msum2[:, 0:1], msum2[:, 1:2], D, 1).then_inc(rstd_ready, 1)

        @block.scalar
        def _(act):
            act.dma_start(ident[:], identity).then_inc(ident_in, 16)
            for r in (0, 2):
                act.dma_start(pair_sum[r:r + 2, :], identity[0:2, 0:2]).then_inc(ident_in, 16)
            act.dma_start(rows[0:16, :], c.rearrange("(r n) -> r n", n=P)).then_inc(vec_in, 16)
            act.dma_start(rows[16:32, :], c_ctx.rearrange("(r n) -> r n", n=P)).then_inc(vec_in, 16)
            act.dma_start(rows[32:48, :], norm1_g.rearrange("(r n) -> r n", n=P)).then_inc(vec_in, 16)
            act.dma_start(rows[48:64, :], norm2_g.rearrange("(r n) -> r n", n=P)).then_inc(vec_in, 16)
            act.dma_start(rows[64:96, :], b_ada[0:2 * D].rearrange("(r n) -> r n", n=P)).then_inc(vec_in, 16)
            act.dma_start(rows[96:128, :], b_ada[3 * D:5 * D].rearrange("(r n) -> r n", n=P)).then_inc(vec_in, 16)

            b0 = misc_wait_full(act, ("vec", 0))
            nc.scalar.activation(cols[:], b0[:, 0:P], ACT.Copy).then_inc(misc_free[MISC_AT["vec", 0][0]], 1)
            misc_wait_freed(act, ("vec", 0))
            nc.scalar.activation(th[:], cols[:, 0:2 * KT].rearrange("p (v k) -> p v k", v=2), ACT.Tanh, scale=0.5)\
                .then_inc(tanh_ready, 1)
            act.wait_ge(cc_ready, 1)
            nc.scalar.activation(cc4[:, 0:4 * KT].rearrange("p (k v) -> p k v", v=4)[:, :, 0:2], cc[:], ACT.Copy)\
                .then_inc(cc4_hi, 1)

            def split_hi(slot_wait, s, slot, n_raw):
                act.wait_ge(raw_full[s % RAW], n_raw)
                if slot_wait is not None:
                    act.wait_ge(gemm_done, slot_wait)
                nc.scalar.activation(slot, raw[:, s % RAW, :], ACT.Copy).then_inc(wh_done, 1)

            def modulate_hi(k):
                act.wait_ge(gain_ready, k // 2 + 1)
                if k == 6:
                    act.wait_ge(gemm_done, MORE_END)
                for src, dst, vv in ((xhT, hT, 0), (chT, cT, 1)):
                    misc_wait_freed(act, (("x", "c")[vv], k))
                    for f in (2 * k, 2 * k + 1):
                        nc.scalar.activation(dst[0][:, f, :], src[:, f, :], ACT.Identity,
                                             bias=mods[:, 0, f, vv:vv + 1], scale=gain1[:, f, vv:vv + 1])\
                            .then_inc(h_hi, 1)

            def evacuate(name, func, dest, **kw):
                for b in range(4):
                    wait_bank(act, CI[name], LAST[name], b)
                    nc.scalar.activation(dest(b), bank[b][:], func, **kw).then_inc(bank_free, 1)

            def cut(t, col):
                return lambda b: t[:, b % 2, col + b // 2 * HC:col + (b // 2 + 1) * HC]

            def squares(src, junk, total, seen, n):
                for h in range(4):
                    if n + h:
                        act.wait_ge(seen, n + h)
                    nc.scalar.activation(junk(h), src(h), ACT.Square, accum_out=total(h)).then_inc(seen, 1)

            def post(m):
                name, k = TILES[m]
                if m in X_IN:
                    n = X_IN[m]
                    t, source = ((xt, x), (ct, ctx_))[n // 2]
                    act.dma_start(t[:, n % 2, :], source[n % 2 * P:(n % 2 + 1) * P, :]).then_inc(tokens_in[n], 16)
                if m == TAB_K - AHEAD:
                    act.dma_start(ropeC[:], rope_c.rearrange("(b p) n -> p b n", p=P)).then_inc(rope_in, 16)
                    act.dma_start(ropeS[:], rope_s.rearrange("(b p) n -> p b n", p=P)).then_inc(rope_in, 16)
                    act.dma_start(gq[:, 0, :], q_norm_g.partition_broadcast(P)).then_inc(rope_in, 16)
                    act.dma_start(gq[:, 1, :], k_norm_g.partition_broadcast(P)).then_inc(rope_in, 16)
                if m in SQX:
                    n = SQX[m]
                    t = (xt, ct)[n // 2]
                    act.wait_ge(tokens_in[n], 16)
                    if n:
                        act.wait_ge(sqx_ready, n)
                    nc.scalar.activation(junk_x[:], t[:, n % 2, :], ACT.Square, accum_out=ssx[:, n:n + 1])\
                        .then_inc(sqx_ready, 1)
                if name in MODS and m == LAST[name]:
                    p = MODS.index(name)
                    act.wait_ge(gemm_done, m + 1)
                    if p >= 2:
                        misc_wait_full(act, ("mod", p - 2))
                    nc.scalar.activation(modrow[:, p % 2, :], bank[MOD_BANK[name[0]]][0:4, :], ACT.Copy)\
                        .then_inc(modrow_ready, 1)
                if m in XTR:
                    key = XTR[m]
                    b = misc_wait_full(act, key)
                    dst = {"x": xhT, "c": chT}[key[0]]
                    nc.scalar.activation(dst[:, 2 * key[1]:2 * key[1] + 2, :].rearrange("p f t -> p (f t)"), b[:],
                                         ACT.Copy).then_inc(misc_free[MISC_AT[key][0]], 1)
                if m == FIRST["V"]:
                    act.dma_start(dft_sb[:], dft.rearrange("(b p) n -> p b n", p=P)).then_inc(dft_in, 16)
                if m == LAST["K"]:
                    misc_wait_freed(act, ("x", 7))
                    evacuate("K", ACT.Copy, lambda b: kraw[:, b, :])
                if 0 <= m - LAST["K"] - 1 < 4:
                    t = m - LAST["K"] - 1
                    if t == 0:
                        act.wait_ge(bank_free, 4 * CI["K"] + 4)
                        act.wait_ge(const_set, 3)
                    squares(lambda h: kraw[:, t, h * HD:(h + 1) * HD], lambda h: krot[:, t, h * HD:(h + 1) * HD],
                            lambda h: ssk[:, 4 * t + h:4 * t + h + 1],
                            sqk_ready, 4 * t)
                if m == LAST["V"]:
                    misc_wait_freed(act, ("c", 7))
                    evacuate("V", ACT.Copy, lambda b: v[:, b, :])
                if m in KTR:
                    t = KTR[m]
                    b = misc_wait_full(act, ("k", t))
                    nc.scalar.activation(kT[:, :, t * P:(t + 1) * P], b[:].rearrange("p (h t) -> p h t", h=NKV),
                                         ACT.Copy).then_inc(misc_free[MISC_AT["k", t][0]], 1)
                if m == LAST["F"]:
                    evacuate("F", ACT.Copy, cut(fin, 0))
                if m in FOUR1:
                    d = FOUR1[m]
                    b = misc_wait_full(act, ("four1", d))
                    nc.scalar.activation(ab[:, d, :], b[:], ACT.Copy).then_inc(misc_free[MISC_AT["four1", d][0]], 1)
                if m in FOUR2:
                    g = FOUR2[m]
                    b = misc_wait_full(act, ("four2", g))
                    nc.scalar.activation(yT[0][:, 2 * g:2 * g + 2, :].rearrange("p f t -> p (f t)"), b[:], ACT.Copy)\
                        .then_inc(hi_done, 1)
                for ch in range(2):
                    if m == LAST[f"Q{ch}"]:
                        if ch:
                            act.wait_ge(qr_ready, 4)
                        evacuate(f"Q{ch}", ACT.Copy, cut(qraw, 0))
                    if m in SQ_Q and SQ_Q[m][0] == ch:
                        g = SQ_Q[m][1]
                        if g == 0:
                            act.wait_ge(bank_free, 4 * CI[f"Q{ch}"] + 4)
                            if ch == 0:
                                act.wait_ge(sqk_ready, 16)
                        squares(lambda h: qraw[:, g // 2, (g % 2 * 4 + h) * HD:(g % 2 * 4 + h + 1) * HD],
                                lambda h: qrot[:, g // 2, (g % 2 * 4 + h) * HD:(g % 2 * 4 + h + 1) * HD],
                                lambda h: ssq[:, ch, 4 * g + h:4 * g + h + 1], sqq_ready, 16 * ch + 4 * g)
                if m in QTR:
                    ch, g = QTR[m]
                    b = misc_wait_full(act, ("q", (ch, g)))
                    h0 = 8 * ch + g % 2 * 4
                    nc.scalar.activation(qT[:, h0:h0 + 4, g // 2 * P:(g // 2 + 1) * P],
                                         b[:].rearrange("p (h t) -> p h t", h=4), ACT.Copy)\
                        .then_inc(misc_free[MISC_AT["q", (ch, g)][0]], 1)
                if m in SLOTS:
                    u = SLOTS[m]
                    if u < UNITS:
                        h, t = divmod(u, TB)
                        col = 8 * t + h % 8
                        act.wait_ge(nb_ready, u + 1)
                        if u >= 2:
                            act.wait_ge(pt_full, u - 1)
                        nc.scalar.activation(probs[:, u % 2, :], bank[4][:], ACT.Exp, bias=nb[:, u:u + 1],
                                             scale=qs[:, h // 8, col:col + 1], accum_out=rsum[:, u:u + 1])\
                            .then_inc(exp_done, 1)
                    if 2 <= u < UNITS + 2:
                        w = u - 2
                        act.wait_ge(pt_full, w + 1)
                        if w >= 2:
                            act.wait_ge(pv_done, w - 1)
                        nc.scalar.activation(probsT[:, w % 2, :, :].rearrange("p k q -> p (k q)"), bank[6][:], ACT.Copy)\
                            .then_inc(pt_ready, 1)
                    if 3 <= u:
                        w = u - 3
                        h, t = divmod(w, TB)
                        act.wait_ge(pv_done, w + 1)
                        nc.scalar.activation(oT[:, h, t * P:(t + 1) * P], bank[7][:, 0:P], ACT.Copy)\
                            .then_inc(o_ready, 1)
                for ch in range(2):
                    if m == LAST[f"GA{ch}"]:
                        if ch == 0:
                            misc_wait_full(act, ("q", (1, 3)))
                        evacuate(f"GA{ch}", ACT.Tanh, cut(gateA, ch * NC), scale=0.5)
                    if m == LAST[f"GF{ch}"]:
                        evacuate(f"GF{ch}", ACT.Tanh, cut(gateF, ch * NC), scale=0.5)
                if m in OH:
                    g = OH[m]
                    act.wait_ge(s_done, UNITS)
                    act.wait_ge(o_ready, 8 * (g + 1))
                    nc.scalar.activation(oS[0][:, 4 * g:4 * g + 4, :], oT[:, 4 * g:4 * g + 4, :], ACT.Copy)\
                        .then_inc(hi_done, 1)
                if m in MTR:
                    ch, g = MTR[m]
                    b = misc_wait_full(act, ("m", (ch, g)))
                    f = 8 * ch + 2 * g
                    nc.scalar.activation(mT[0][:, f:f + 2, :].rearrange("p f t -> p (f t)"), b[:], ACT.Copy, scale=0.5)\
                        .then_inc(hi_done, 1)
                for ch in range(2):
                    if m == LAST[f"O{ch}"]:
                        for i, b in enumerate(ROWS_FIRST if ch else range(4)):
                            n = 4 * ch + i
                            act.wait_ge(x1_ready, n + 1)
                            if n:
                                act.wait_ge(sq1_ready, n)
                            nc.scalar.activation(junk_1[:, b, :], cut(x1, ch * NC)(b), ACT.Square,
                                                 accum_out=ss1[:, b % 2, 2 * ch + b // 2:2 * ch + b // 2 + 1])\
                                .then_inc(sq1_ready, 1)
                            for key in {1: GATE2[:1], 2: GATE2[1:2], 3: GATE2[2:]}.get(i, []) if ch else []:
                                _, jc, half = key
                                bank_g = misc_wait_full(act, key)
                                nc.scalar.activation(acc[:, jc % 2, half * HC:(half + 1) * HC], bank_g[:], ACT.Copy)\
                                    .then_inc(misc_free[MISC_AT[key][0]], 1)

            def modulate2_hi(g):
                b = misc_wait_full(act, ("xs", g))
                for j in range(2):
                    f = 2 * g + j
                    nc.scalar.activation(h2T[0][:, f, :], b[:, j * T:(j + 1) * T], ACT.Identity,
                                         bias=mods2[:, 0, f:f + 1], scale=gain2[:, f:f + 1]).then_inc(hi_done, 1)

            for m, (name, k) in enumerate(TILES):
                s = STREAM_AT["M", m]
                split_hi(None if BEFORE[m] is None else BEFORE[m] + 1, s, hi_slot(m), 16 * (s // RAW + 1))
                for before in POSTS.get(m, []):
                    post(before)
                if m in MODULATE:
                    modulate_hi(MODULATE[m])

            def hi_1(i, k):
                s = S1 + k
                split_hi(i * KT + (M1 + k - SPL + 1), s, wh[:, k % SPL, :], i * (16 * KT // RAW) + 16 * (s // RAW + 1))

            def hidden(i, g):
                act.wait_ge(hT_full, i * 4 + (g + 1))
                nc.scalar.activation(hid[:, bass.ds(i * 8 + 2 * g, 2), :], bank[4 + g][:].rearrange("p (f t) -> p f t", f=2),
                                     ACT.Square).then_inc(hid_ready, 1)

            for k in range(KT):
                hi_1(0, k)
                if k < AHEAD:
                    post(M1 - AHEAD + k)
                if k == AHEAD - 1:
                    for g in range(XS_NOW):
                        modulate2_hi(g)
                if AHEAD <= k and XS_NOW + k - AHEAD < 8:
                    modulate2_hi(XS_NOW + k - AHEAD)
            with nc.scalar.Fori(1, N1) as i:
                for k in range(KT):
                    hi_1(i, k)
                    if 3 <= k < 7:
                        hidden(i - 1, k - 3)

            def hi_2(g, j):
                s = S1 + j
                if j % 4 == 0:
                    q = j // 4
                    if not (isinstance(g, int) and g == 0):
                        act.wait_ge(gemm_done, g * 8 + (M2 + j - 4))
                    nc.scalar.activation(hidS[0][:, q, :, :], hid[:, bass.ds(g * 4 + 2 * q, 2), :], ACT.Copy)\
                        .then_inc(hs_hi, 1)
                split_hi(g * 8 + (M2 + j - SPL + 1), s, wh[:, j % SPL, :],
                         g * (16 * 8 // RAW) + 16 * ((s + (M2 - M1)) // RAW + 1))

            for j in range(8):
                hi_2(0, j)
                if j == 1:
                    for g in range(4):
                        hidden(N1 - 1, g)
            with nc.scalar.Fori(1, N2 // 8) as g:
                for j in range(8):
                    hi_2(g, j)
            for i, b in enumerate(LAST_BANKS):
                n, half, t = b // 4, b // 2 % 2, b % 2
                wait_x2(act, i)
                if i:
                    act.wait_ge(sq2_ready, i)
                nc.scalar.activation(junk_2[:, b, :], x1[:, t, n * NC + half * HC:n * NC + (half + 1) * HC], ACT.Square,
                                     accum_out=ss2[:, t, 2 * n + half:2 * n + half + 1]).then_inc(sq2_ready, 1)

        @block.vector
        def _(dve):
            steps = [0]

            def then(ins):
                steps[0] += 1
                ins.then_inc(dve_step, 1)
                dve.wait_ge(dve_step, steps[0])

            dve.wait_ge(tanh_ready, 1)
            then(nc.vector.tensor_scalar(th[:], th[:], 1.0, 0.5, ALU.add, ALU.mult))
            nc.vector.tensor_tensor(cc[:].rearrange("p k v -> p v k"), th[:],
                                    cols[:, 0:2 * KT].rearrange("p (v k) -> p v k", v=2), ALU.mult).then_inc(cc_ready, 1)
            dve.wait_ge(cc4_hi, 1)
            cc4_k = cc4[:, 0:4 * KT].rearrange("p (k v) -> p k v", v=4)
            nc.vector.tensor_tensor(cc4_k[:, :, 2:4], cc[:], cc4_k[:, :, 0:2].bitcast(F32), ALU.subtract)\
                .then_inc(cc4_ready, 1)

            def rope_tables(which):
                pair = gq[:, which, :].rearrange("p (j two) -> p j two", two=2)
                for t in range(TB):
                    then(nc.vector.tensor_tensor(tabC[:, t, :], ropeC[:, t, :], gq[:, which, :], ALU.mult))
                    s_in = ropeS[:, t, :].rearrange("p (j two) -> p j two", two=2)
                    s_out = tabS[:, t, :].rearrange("p (j two) -> p j two", two=2)
                    for e in range(2):
                        then(nc.vector.tensor_tensor(s_out[:, :, e], s_in[:, :, e], pair[:, :, 1 - e], ALU.mult))

            def mod_columns(p):
                quarter, kind = divmod(p, 2)
                b = misc_wait_full(dve, ("mod", p))
                f = slice(4 * quarter, 4 * quarter + 4)
                bias = cols[:, 64 + 16 * kind + 4 * quarter:68 + 16 * kind + 4 * quarter]
                mine = b[:, 0:8].rearrange("p (f v) -> p f v", v=2)
                for vv in range(2):
                    ins = nc.vector.tensor_tensor(mods[:, kind, f, vv], mine[:, :, vv], bias, ALU.add)
                    if vv == 0:
                        then(ins)
                ins.then_inc(misc_free[MISC_AT["mod", p][0]], 1)
                if kind == 1:
                    misc_wait_freed(dve, ("mod", p))
                    for vv in range(2):
                        g = cols[:, 32 + 4 * quarter:36 + 4 * quarter]
                        ins = nc.vector.scalar_tensor_tensor(gain1[:, f, vv], mods[:, 1, f, vv], 1.0, g, ALU.add, ALU.mult)
                        if vv == 0:
                            then(ins)
                    ins.then_inc(gain_ready, 1)

            def modulate_lo(k):
                for vv, dst in enumerate((hT, cT)):
                    n = 2 * k + vv
                    dve.wait_ge(h_tmp, 2 * n + 2)
                    dve.wait_ge(h_hi, 2 * n + 2)
                    nc.vector.tensor_tensor(dst[1][:, 2 * k:2 * k + 2, :], hmod[:, vv, :, :],
                                            dst[0][:, 2 * k:2 * k + 2, :].bitcast(F32), ALU.subtract).then_inc(h_lo, 1)

            def split_lo(n_wh, s, hi, lo):
                dve.wait_ge(wh_done, n_wh)
                nc.vector.tensor_tensor(lo, raw[:, s % RAW, :], hi.bitcast(F32), ALU.subtract)\
                    .then_inc(wl_done, 1)

            def mac(j):
                jc, k = divmod(j, KT)
                s = STREAM.index(("A", jc, k))
                dve.wait_ge(raw_full[s % RAW], 16 * (s // RAW + 1))
                if k == 0:
                    if jc == 0:
                        dve.wait_ge(gemm_done, MODS_END)
                        misc_wait_full(dve, ("mod", 7))
                    if jc >= 2:
                        misc_wait_full(dve, ("ada", jc - 2, 0 if jc < 6 else 1))
                    nc.vector.tensor_scalar(acc[:, jc % 2, :], raw[:, s % RAW, :], cc[:, k, 0:1], None, ALU.mult)\
                        .then_inc(mac_step, 1)
                else:
                    dve.wait_ge(mac_step, j)
                    nc.vector.scalar_tensor_tensor(acc[:, jc % 2, :], raw[:, s % RAW, :], cc[:, k, 0:1], acc[:, jc % 2, :],
                                                   ALU.mult, ALU.add).then_inc(mac_step, 1)

            def rotate(src, dst, t, n):
                c_b = tabC[:, t, :].unsqueeze(1).to_broadcast([P, n, HD])
                s_b = tabS[:, t, :].rearrange("p (j two) -> p j two", two=2)
                s4 = src.rearrange("p (h j two) -> p h j two", h=n, two=2)
                d4 = dst.rearrange("p (h j two) -> p h j two", h=n, two=2)
                for e in range(2):
                    then(nc.vector.tensor_tensor(d4[:, :, :, e], s4[:, :, :, 1 - e],
                                                 s_b[:, :, e].unsqueeze(1).to_broadcast([P, n, HD // 2]), ALU.mult))
                s3 = src.rearrange("p (h d) -> p h d", h=n)
                then(nc.vector.tensor_tensor(s3, s3, c_b, ALU.mult))
                return nc.vector.tensor_tensor(dst, dst, src, ALU.add)

            def cut(t, col):
                return lambda b: t[:, b % 2, col + b // 2 * HC:col + (b // 2 + 1) * HC]

            def post(m):
                if m in XN:
                    n = XN[m]
                    dve.wait_ge(rstd_ready, 1)
                    t = (xt, ct)[n // 2]
                    nc.vector.tensor_scalar(t[:, n % 2, :], t[:, n % 2, :], rsx[:, n:n + 1], None, ALU.mult)\
                        .then_inc(xn_ready, 1)
                if m == TAB_K:
                    dve.wait_ge(rope_in, 64)
                    rope_tables(1)
                if m in ADA_SUM:
                    jc = ADA_SUM[m]
                    if jc < 4:
                        kind, half = divmod(jc, 2)
                        b = misc_wait_full(dve, ("ada", jc, 0))
                        f = slice(8 * half, 8 * half + 8)
                        nc.vector.tensor_tensor(mods2[:, kind, f], b[:, 0:8],
                                                cols[:, 96 + 16 * kind + 8 * half:104 + 16 * kind + 8 * half], ALU.add)\
                            .then_inc(misc_free[MISC_AT["ada", jc, 0][0]], 1)
                        if kind == 1:
                            misc_wait_freed(dve, ("ada", jc, 0))
                            nc.vector.scalar_tensor_tensor(gain2[:, f], mods2[:, 1, f], 1.0,
                                                           cols[:, 48 + 8 * half:56 + 8 * half], ALU.add, ALU.mult)\
                                .then_inc(g_done, 1)
                    else:
                        dve.wait_ge(g1_in, 16)
                        for half in range(2):
                            b = misc_wait_full(dve, ("ada", jc, half))
                            col = jc % 2 * NC + half * HC
                            nc.vector.tensor_tensor(g1row[:, col:col + HC], g1row[:, col:col + HC], b[:], ALU.add)\
                                .then_inc(misc_free[MISC_AT["ada", jc, half][0]], 1)
                t = m - LAST["K"] - 3
                if 0 <= t < 4:
                    src, dst = kraw[:, t, :], krot[:, t, :]
                    dve.wait_ge(sqk_ready, 4 * (t + 1))
                    s3 = src.rearrange("p (h d) -> p h d", h=NKV)
                    d3 = dst.rearrange("p (h d) -> p h d", h=NKV)
                    if t < TB:
                        then(rotate(src, dst, t, NKV))
                    else:
                        then(nc.vector.tensor_tensor(d3, s3, gq[:, 1, :].unsqueeze(1).to_broadcast([P, NKV, HD]), ALU.mult))
                    if t == 3:
                        dve.wait_ge(rstd_ready, 2)
                        for w in range(4):
                            w3 = krot[:, w, :].rearrange("p (h d) -> p h d", h=NKV)
                            nc.vector.tensor_tensor(w3, w3, rsk[:, 4 * w:4 * w + 4].unsqueeze(2).to_broadcast([P, NKV, HD]),
                                                    ALU.mult).then_inc(kn_ready, 1)
                        rope_tables(0)
                if m in FOUR2:
                    g = FOUR2[m]
                    b = misc_wait_full(dve, ("four2", g))
                    dve.wait_ge(hi_done, HI_AT["f", g])
                    nc.vector.tensor_tensor(yT[1][:, 2 * g:2 * g + 2, :].rearrange("p f t -> p (f t)"), b[:],
                                            yT[0][:, 2 * g:2 * g + 2, :].rearrange("p f t -> p (f t)").bitcast(F32),
                                            ALU.subtract).then_inc(misc_free[MISC_AT["four2", g][0]], 1)
                if m in ROPE_Q:
                    ch, g = ROPE_Q[m]
                    t, half = divmod(g, 2)
                    dve.wait_ge(sqq_ready, 16 * ch + 4 * (g + 1))
                    if ch:
                        misc_wait_full(dve, ("q", (0, 3)))
                    cols_q = slice(half * HC, (half + 1) * HC)
                    rotate(qraw[:, t, cols_q], qrot[:, t, cols_q], t, 4).then_inc(qr_ready, 1)
                if m in SLOTS:
                    u = SLOTS[m]
                    if u < UNITS:
                        h, t = divmod(u, TB)
                        col = 8 * t + h % 8
                        dve.wait_ge(s_done, u + 1)
                        then(nc.vector.tensor_reduce(mx[:, u:u + 1], bank[4][:], AX.X, ALU.max))
                        dve.wait_ge(rstd_ready, 3 + h // 8)
                        nc.vector.tensor_tensor(nb[:, u:u + 1], mx[:, u:u + 1], nqs[:, h // 8, col:col + 1], ALU.mult)\
                            .then_inc(nb_ready, 1)
                    if 1 <= u < UNITS + 1:
                        w = u - 1
                        dve.wait_ge(exp_done, w + 1)
                        then(nc.vector.reciprocal(rinv[:, w:w + 1], rsum[:, w:w + 1]))
                        nc.vector.tensor_scalar(probs[:, w % 2, :], probs[:, w % 2, :], rinv[:, w:w + 1], None, ALU.mult)\
                            .then_inc(pn_ready, 1)
                if m in OL:
                    g = OL[m]
                    dve.wait_ge(pv_done, UNITS)
                    dve.wait_ge(hi_done, HI_AT["o", g])
                    nc.vector.tensor_tensor(oS[1][:, 4 * g:4 * g + 4, :], oT[:, 4 * g:4 * g + 4, :],
                                            oS[0][:, 4 * g:4 * g + 4, :].bitcast(F32), ALU.subtract).then_inc(ol_done, 1)
                for ch in range(2):
                    if m == LAST[f"A{ch}"]:
                        dve.wait_ge(bank_free, 4 * CI["GF1"] + 4)
                        for b in range(4):
                            wait_bank(dve, CI[f"A{ch}"], m, b)
                            part = cut(gateA, ch * NC)(b)
                            nc.vector.scalar_tensor_tensor(part, part, 1.0, bank[b][:], ALU.add, ALU.mult)\
                                .then_inc(bank_free, 1)
                    if m == LAST[f"B{ch}"]:
                        for b in range(4):
                            wait_bank(dve, CI[f"B{ch}"], m, b)
                            part = cut(gateF, ch * NC)(b)
                            nc.vector.scalar_tensor_tensor(part, part, 1.0, bank[b][:], ALU.add, ALU.mult)\
                                .then_inc(bank_free, 1)
                        for b in range(4):
                            dve.wait_ge(bank_free, 4 * CI[f"B{ch}"] + b + 1)
                            part = cut(gateA, ch * NC)(b)
                            nc.vector.tensor_tensor(part, part, cut(gateF, ch * NC)(b), ALU.add).then_inc(mid_done, 1)
                    if m == LAST[f"O{ch}"]:
                        dve.wait_ge(xr_in, 16)
                        for i, b in enumerate(ROWS_FIRST if ch else range(4)):
                            wait_bank(dve, CI[f"O{ch}"], m, i)
                            col = ch * NC + b // 2 * HC
                            if ch:
                                dve.wait_ge(x1_ready, i + 1)
                            nc.vector.tensor_tensor(scr[:, i, :], bank[b][:], g1row[:, col:col + HC], ALU.mult)\
                                .then_inc(bank_free, 1)
                            dve.wait_ge(bank_free, 4 * CI[f"O{ch}"] + i + 1)
                            part = cut(x1, ch * NC)(b)
                            nc.vector.tensor_tensor(part, part, scr[:, i, :], ALU.add).then_inc(x1_ready, 1)
                if m in MTR:
                    ch, g = MTR[m]
                    b = misc_wait_full(dve, ("m", (ch, g)))
                    dve.wait_ge(hi_done, HI_AT["m", (ch, g)])
                    f = 8 * ch + 2 * g
                    nc.vector.scalar_tensor_tensor(mT[1][:, f:f + 2, :].rearrange("p f t -> p (f t)"), b[:], 0.5,
                                                   mT[0][:, f:f + 2, :].rearrange("p f t -> p (f t)").bitcast(F32),
                                                   ALU.mult, ALU.subtract)\
                        .then_inc(misc_free[MISC_AT["m", (ch, g)][0]], 1)

            def modulate2_lo(g):
                b = misc_wait_full(dve, ("xs", g))
                dve.wait_ge(hi_done, HI_AT["xs", 2 * g + 1])
                if g >= 2:
                    misc_wait_freed(dve, ("xs", g - 2))
                for j in range(2):
                    f = 2 * g + j
                    then(nc.vector.tensor_scalar(hmod2[:, g % 2, j, :], b[:, j * T:(j + 1) * T], gain2[:, f:f + 1],
                                                 mods2[:, 0, f:f + 1], ALU.mult, ALU.add))
                nc.vector.tensor_tensor(h2T[1][:, 2 * g:2 * g + 2, :], hmod2[:, g % 2, :, :],
                                        h2T[0][:, 2 * g:2 * g + 2, :].bitcast(F32), ALU.subtract)\
                    .then_inc(misc_free[MISC_AT["xs", g][0]], 1)

            for m, (name, k) in enumerate(TILES):
                split_lo(m + 1, STREAM_AT["M", m], hi_slot(m), lo_slot(m))
                if m in MOD_ADD:
                    mod_columns(MOD_ADD[m])
                if m in MODULATE:
                    if MODULATE[m] == 6:
                        mod_columns(7)
                    modulate_lo(MODULATE[m])
                for j in ADA_AT[m]:
                    mac(j)
                for before in POSTS.get(m, []):
                    post(before)

            def lo_1(i, k):
                split_lo(i * KT + (M1 + k + 1), S1 + k, wh[:, k % SPL, :], wl[:, k % SPL, :])

            def relu(i):
                for b in range(4):
                    if b < 3:
                        dve.wait_ge(bank_full, i * 3 + (3 * CI1 + b + 1))
                    else:
                        dve.wait_ge(gemm_done, i * KT + (M1 + KT))
                    if b == 0:
                        if not (isinstance(i, int) and i == 0):
                            dve.wait_ge(hT_full, i * 4)
                    nc.vector.tensor_scalar(hs[:, b % 2, b // 2 * HC:(b // 2 + 1) * HC], bank[b][:], 0.0, None, ALU.max)\
                        .then_inc(bank_free, 1)

            for k in range(KT):
                lo_1(0, k)
                if k < AHEAD:
                    post(M1 - AHEAD + k)
                if k == AHEAD - 1:
                    for t in range(TB):
                        dve.wait_ge(rstd_ready, 5 + t)
                        for half in range(2):
                            nc.vector.tensor_scalar(xs[:, t, half * NC:(half + 1) * NC], x1[:, t, half * NC:(half + 1) * NC],
                                                    rs1[:, t:t + 1], None, ALU.mult).then_inc(xs_ready, 1)
                    dve.wait_ge(g_done, 2)
                    for g in range(XS_NOW):
                        modulate2_lo(g)
                if AHEAD <= k and XS_NOW + k - AHEAD < 8:
                    modulate2_lo(XS_NOW + k - AHEAD)
                if k in (10, 12):
                    half = (k - 10) // 2
                    dve.wait_ge(g2_in, 16)
                    for key in GATE2[2 * half:2 * half + 2]:
                        misc_wait_freed(dve, key)
                    part = g2row[:, half * NC:(half + 1) * NC]
                    then(nc.vector.tensor_tensor(part, part, acc[:, half, :], ALU.add))
            with nc.vector.Fori(1, N1) as i:
                for k in range(KT):
                    lo_1(i, k)
                    if k == 1:
                        relu(i - 1)

            def lo_2(g, j):
                if j % 4 == 0:
                    q = j // 4
                    dve.wait_ge(hs_hi, g * 2 + (q + 1))
                    nc.vector.tensor_tensor(hidS[1][:, q, :, :], hid[:, bass.ds(g * 4 + 2 * q, 2), :],
                                            hidS[0][:, q, :, :].bitcast(F32), ALU.subtract).then_inc(hs_lo, 1)
                split_lo(g * 8 + (M2 + j + 1), S1 + j, wh[:, j % SPL, :], wl[:, j % SPL, :])

            for j in range(8):
                lo_2(0, j)
                if j == 1:
                    relu(N1 - 1)
            with nc.vector.Fori(1, N2 // 8) as g:
                for j in range(8):
                    lo_2(g, j)
            for i, b in enumerate(LAST_BANKS):
                dve.wait_ge(z_full, i + 1)
                col = b // 2 * HC
                ins = nc.vector.tensor_tensor(scr2[:, b, :], bank[b][:], g2row[:, col:col + HC], ALU.mult)
                if i in POOL_ADDS:
                    ins.then_inc(gz_ready, 1)
                    continue
                then(ins)
                nc.vector.tensor_tensor(last_part(x1, b), last_part(x1, b), scr2[:, b, :], ALU.add).then_inc(x2_ready, 1)
            dve.wait_ge(fg_in, 16)
            wait_x2(dve, 7)
            for t in range(TB):
                dve.wait_ge(rstd_ready, 7 + t)
                wait_x2(dve, POOL_ADDS[-1])
                for half in range(2):
                    part = slice(half * NC, (half + 1) * NC)
                    nc.vector.scalar_tensor_tensor(res[:, t, part], x1[:, t, part], rs2[:, t:t + 1], fgrow[:, part],
                                                   ALU.mult, ALU.mult).then_inc(res_ready, 1)

        @block.tensor
        def _(pe):
            def misc_take(key):
                b, n = MISC_AT[key]
                if n:
                    pe.wait_ge(misc_free[b], n)
                return bank[b], misc_full[b]

            def products(b, terms, start, stop):
                for j, (a_hi, a_lo, w_hi, w_lo) in enumerate(terms):
                    first, last = start and j == 0, stop and j == len(terms) - 1
                    nc.tensor.matmul(bank[b][:], a_hi, w_hi, start=first, stop=False)
                    nc.tensor.matmul(bank[b][:], a_hi, w_lo, start=False, stop=False)
                    ins = nc.tensor.matmul(bank[b][:], a_lo, w_hi, start=False, stop=last)
                return ins

            def tile_products(a, k, slot, banks, start, stop, free=None):
                for n, b in enumerate(banks):
                    half, t = n // 2, n % 2
                    if free is not None:
                        pe.wait_ge(bank_free, free + n)
                    w = slice(half * HC, (half + 1) * HC)
                    cols_t = slice(t * P, (t + 1) * P)
                    ins = products(b, [(a[0][:, k, cols_t], a[1][:, k, cols_t], wh[:, slot, w], wl[:, slot, w])], start, stop)
                    if n == 3:
                        ins.then_inc(gemm_done, 1)
                    elif stop:
                        ins.then_inc(bank_full, 1)

            pe.wait_ge(ident_in, 48)
            pe.wait_ge(vec_in, 96)
            pe.wait_ge(const_set, 3)
            b, full = misc_take(("vec", 0))
            nc.tensor.transpose(b[:, 0:P], rows[:], ident[:]).then_inc(full, 1)
            pe.wait_ge(cc4_ready, 1)

            def token_transposes(key, src, f0):
                b, full = misc_take(key)
                for n in range(4):
                    f, t = f0 + n // 2, n % 2
                    ins = nc.tensor.transpose(b[:, n * P:(n + 1) * P], src[:, t, f * P:(f + 1) * P], ident[:])
                ins.then_inc(full, 1)

            def hook(m):
                if m in MOD_COLS:
                    p = MOD_COLS[m]
                    pe.wait_ge(modrow_ready, p + 1)
                    b, full = misc_take(("mod", p))
                    for f in range(4):
                        ins = nc.tensor.matmul(b[:, 2 * f:2 * f + 2], modrow[:, p % 2, f * P:(f + 1) * P], pair_sum[:],
                                               start=True, stop=True)
                    ins.then_inc(full, 1)
                if m in XTR:
                    key = XTR[m]
                    pe.wait_ge(xn_ready, {"x": 2, "c": 4}[key[0]])
                    token_transposes(key, {"x": xt, "c": ct}[key[0]], 2 * key[1])
                if m in ADA_SUM:
                    jc = ADA_SUM[m]
                    pe.wait_ge(mac_step, KT * (jc + 1))
                    if jc < 4:
                        b, full = misc_take(("ada", jc, 0))
                        for f in range(8):
                            ins = nc.tensor.matmul(b[:, f:f + 1], acc[:, jc % 2, f * P:(f + 1) * P], ones[:, 0:1],
                                                   start=True, stop=True)
                        ins.then_inc(full, 1)
                    else:
                        for half in range(2):
                            b, full = misc_take(("ada", jc, half))
                            nc.tensor.matmul(b[:], ones[:], acc[:, jc % 2, half * HC:(half + 1) * HC],
                                             start=True, stop=True).then_inc(full, 1)
                if m in KTR:
                    t = KTR[m]
                    pe.wait_ge(kn_ready, t + 1)
                    b, full = misc_take(("k", t))
                    for h in range(NKV):
                        ins = nc.tensor.transpose(b[:, h * P:(h + 1) * P], krot[:, t, h * HD:(h + 1) * HD], ident[:])
                    ins.then_inc(full, 1)
                if m in FOUR1:
                    d = FOUR1[m]
                    if d == 0:
                        pe.wait_ge(dft_in, 16)
                    b, full = misc_take(("four1", d))
                    for t in range(TB):
                        ins = nc.tensor.matmul(b[:], fin[:, t, d * P:(d + 1) * P], dft_sb[:, t, 0:2 * FG],
                                               start=(t == 0), stop=(t == TB - 1))
                    ins.then_inc(full, 1)
                if m in FOUR2:
                    g = FOUR2[m]
                    if g == 0:
                        for d in range(8):
                            misc_wait_freed(pe, ("four1", d))
                    b, full = misc_take(("four2", g))
                    for o in range(2):
                        for e in range(2):
                            for part, tab in ((0, 0), (1, 2 * FG)):
                                ins = nc.tensor.matmul(b[:, o * T:(o + 1) * T], dft_sb[:, e, tab + o * P:tab + (o + 1) * P],
                                                       ab[:, 2 * g + e, part * T:(part + 1) * T],
                                                       start=(e == 0 and part == 0), stop=(e == 1 and part == 1))
                    ins.then_inc(full, 1)
                if m in QTR:
                    ch, g = QTR[m]
                    t, half = divmod(g, 2)
                    pe.wait_ge(qr_ready, 4 * ch + g + 1)
                    b, full = misc_take(("q", (ch, g)))
                    for h in range(4):
                        col = half * HC + h * HD
                        ins = nc.tensor.transpose(b[:, h * P:(h + 1) * P], qrot[:, t, col:col + HD], ident[:])
                    ins.then_inc(full, 1)
                if m in SLOTS:
                    u = SLOTS[m]
                    if u == 0:
                        for t in range(4):
                            misc_wait_freed(pe, ("k", t))
                        pe.wait_ge(bank_free, 4 * CI["V"] + 4)
                        for bb in (6, 7):
                            pe.wait_ge(misc_free[bb], max(n + 1 for key, (x_, n) in MISC_AT.items()
                                                          if x_ == bb and MISC.index(key) < _busy_from))
                    if u < UNITS:
                        h, t = divmod(u, TB)
                        if h % 8 == 0 and t == 0:
                            for g in range(4):
                                misc_wait_freed(pe, ("q", (h // 8, g)))
                        if u:
                            pe.wait_ge(exp_done, u)
                        nc.tensor.matmul(bank[4][:], qT[:, h, t * P:(t + 1) * P], kT[:, h // QPK, :],
                                         start=True, stop=True).then_inc(s_done, 1)
                    if 2 <= u < UNITS + 2:
                        w = u - 2
                        pe.wait_ge(pn_ready, w + 1)
                        if w:
                            pe.wait_ge(pt_ready, w)
                        for kb in range(4):
                            ins = nc.tensor.transpose(bank[6][:, kb * P:(kb + 1) * P], probs[:, w % 2, kb * P:(kb + 1) * P],
                                                      ident[:])
                        ins.then_inc(pt_full, 1)
                    if 3 <= u:
                        w = u - 3
                        h, t = divmod(w, TB)
                        pe.wait_ge(pt_ready, w + 1)
                        if w:
                            pe.wait_ge(o_ready, w)
                        for kb in range(4):
                            ins = nc.tensor.matmul(bank[7][:, 0:P], v[:, kb, h // QPK * HD:(h // QPK + 1) * HD],
                                                   probsT[:, w % 2, kb, :], start=(kb == 0), stop=(kb == 3))
                        ins.then_inc(pv_done, 1)
                if m in MTR:
                    ch, g = MTR[m]
                    if ch == 0 and g == 0:
                        pe.wait_ge(o_ready, UNITS)
                    pe.wait_ge(mid_done, 4 * (ch + 1))
                    token_transposes(("m", (ch, g)), gateA, 8 * ch + 2 * g)

            for m, (name, k) in enumerate(TILES):
                last = m == LAST[name]
                if name == "K":
                    pe.wait_ge(h_lo, 2 * (k + 1))
                pe.wait_ge(wl_done, m + 1)
                if name in MODS:
                    p = MODS.index(name)
                    if p >= 2 and k == 0:
                        pe.wait_ge(modrow_ready, p - 1)
                    for j in range(2):
                        for n_part, part in enumerate((hi_slot(m), lo_slot(m))):
                            ins = nc.tensor.matmul(bank[MOD_BANK[name[0]]][:], cc4[:, 4 * (2 * k + j):4 * (2 * k + j) + P],
                                                   part[:, j * HC:(j + 1) * HC],
                                                   start=(k == 0 and j == 0 and n_part == 0),
                                                   stop=(k == KT // 2 - 1 and j == 1 and n_part == 1))
                    ins.then_inc(gemm_done, 1)
                elif name in "KV":
                    for t in range(4):
                        if k == 0:
                            if name == "V":
                                pe.wait_ge(bank_free, 4 * CI["K"] + t + 1)
                        a = hT if t < TB else cT
                        cols_t = slice(t % 2 * P, (t % 2 + 1) * P)
                        ins = products(t, [(a[0][:, 2 * k + j, cols_t], a[1][:, 2 * k + j, cols_t],
                                            hi_slot(m)[:, j * HC:(j + 1) * HC], lo_slot(m)[:, j * HC:(j + 1) * HC])
                                           for j in range(2)], k == 0, last)
                        if t == 3:
                            ins.then_inc(gemm_done, 1)
                        elif last:
                            ins.then_inc(bank_full, 1)
                else:
                    a = {"A": oS, "B": yT, "O": mT}.get(name[0], hT)
                    if name[0] == "A" and k % 4 == 0:
                        pe.wait_ge(ol_done, k // 4 + 1)
                    if name == "B0" and k == 0:
                        for g in range(4):
                            misc_wait_freed(pe, ("four2", g))
                    if name[0] == "O" and k % 2 == 0 and name == "O0":
                        misc_wait_freed(pe, ("m", divmod(k // 2, 4)))
                    if m == M1 - 2:
                        continue
                    if m == M1 - 1:
                        for i, b in enumerate(ROWS_FIRST):
                            w, cols_t = slice(b // 2 * HC, (b // 2 + 1) * HC), slice(b % 2 * P, (b % 2 + 1) * P)
                            ins = products(b, [(a[0][:, kk, cols_t], a[1][:, kk, cols_t], wh[:, mm % SPL, w], wl[:, mm % SPL, w])
                                               for kk, mm in ((k - 1, m - 1), (k, m))], False, True)
                            if i < 3:
                                ins.then_inc(bank_full, 1)
                        ins.then_inc(gemm_done, 2)
                    else:
                        tile_products(a, k, m % SPL, range(4), k == 0, last, 4 * CI[name] - 3 if k == 0 else None)
                hook(m)

            def xs_transposes(g):
                pe.wait_ge(xs_ready, 3 if g < 4 else 4)
                token_transposes(("xs", g), xs, 2 * g)

            pe.wait_ge(mac_step, KT * 8)
            for key in GATE2:
                _, jc, half = key
                b, full = misc_take(key)
                nc.tensor.matmul(b[:], ones[:], acc[:, jc % 2, half * HC:(half + 1) * HC], start=True, stop=True)\
                    .then_inc(full, 1)
            for g in range(XS_NOW):
                xs_transposes(g)
            pe.wait_ge(bank_free, 4 * CI1)

            def first_product(i, k):
                pe.wait_ge(wl_done, i * KT + (M1 + k + 1))
                if isinstance(i, int) and i == 0 and k % 2 == 0:
                    misc_wait_freed(pe, ("xs", k // 2))
                tile_products(h2T, k, k % SPL, range(4), k == 0, k == KT - 1,
                              i * 4 + (4 * CI1 - 3) if k == 0 else None)

            def hidden_transposes(i, g):
                if g == 0:
                    pe.wait_ge(bank_free, i * 4 + 4 * (CI1 + 1))
                if isinstance(i, int) and i == 0:
                    if g in (1, 2, 3):
                        pe.wait_ge(misc_free[4 + g], _uses[4 + g])
                else:
                    pe.wait_ge(hid_ready, i * 4 + (g - 3))
                for n in range(4):
                    f, t = 2 * g + n // 2, n % 2
                    ins = nc.tensor.transpose(bank[4 + g][:, n * P:(n + 1) * P], hs[:, t, f * P:(f + 1) * P], ident[:])
                ins.then_inc(hT_full, 1)

            for k in range(KT):
                first_product(0, k)
                if XS_NOW + k < 8:
                    xs_transposes(XS_NOW + k)
            for k in range(KT):
                first_product(1, k)
                if 1 <= k < 5:
                    hidden_transposes(0, k - 1)
            with nc.tensor.Fori(2, N1) as i:
                for k in range(KT):
                    first_product(i, k)
                    if 1 <= k < 5:
                        hidden_transposes(i - 1, k - 1)
            for g in range(4):
                hidden_transposes(N1 - 1, g)

            def second_product(g, j, start):
                if j % 4 == 0:
                    pe.wait_ge(hs_lo, g * 2 + (j // 4 + 1))
                pe.wait_ge(wl_done, g * 8 + (M2 + j + 1))
                n = j % 2
                if start and j == 0:
                    pe.wait_ge(bank_free, 4 * (CI1 + N1))
                if start and j == 1:
                    pe.wait_ge(hid_ready, 4 * N1)
                q, e = divmod(j // 2, 2)
                tile_products([hidS[0][:, q, :, :], hidS[1][:, q, :, :]], e, j % SPL, range(4 * n, 4 * n + 4),
                              start and j < 2, False)

            for j in range(8):
                second_product(0, j, True)
            with nc.tensor.Fori(1, N2 // 8 - 1) as g:
                for j in range(8):
                    second_product(g, j, False)
            for j in range(4):
                second_product(N2 // 8 - 1, j, False)
            pe.wait_ge(hs_lo, N2 // 8 * 2)

            def last_products(b, blocks, stop):
                n, w, cols_t = b // 4, slice(b // 2 % 2 * HC, (b // 2 % 2 + 1) * HC), slice(b % 2 * P, (b % 2 + 1) * P)
                return products(b, [(hidS[0][:, 1, e, cols_t], hidS[1][:, 1, e, cols_t], wh[:, 2 * e + n, w],
                                     wl[:, 2 * e + n, w]) for e in blocks], False, stop)

            early = LAST_BANKS[:4]
            for b in early:
                pe.wait_ge(wl_done, M2 + N2 - 3 + b // 4)
                last_products(b, [0], False)
            for b in LAST_BANKS:
                if b in early:
                    pe.wait_ge(wl_done, M2 + N2 - 1 + b // 4)
                last_products(b, [1] if b in early else [0, 1], True).then_inc(z_full, 1)


def constants():
    n = np.arange(T)
    angle = 2 * np.pi * np.outer(n, n) % (2 * np.pi * T) / T
    cos, sin = np.cos(angle) / 16.0, np.sin(angle) / 16.0
    pairs = HD // 4
    inv = 1.0 / (10000.0 ** (np.arange(pairs, dtype=np.float32) / np.float32(pairs)))
    inv = inv.astype(np.float32)
    row = (n // 64).astype(np.float32)[:, None] * inv
    col = (n % 64).astype(np.float32)[:, None] * inv
    ang = np.concatenate([row, col], axis=1).astype(np.float64)
    c, s = np.cos(ang), np.sin(ang)
    return {
        "identity": np.eye(P, dtype=np.float32),
        "dft": np.concatenate([cos, sin, -sin], axis=1).astype(np.float32),
        "rope_c": np.repeat(c, 2, axis=1).astype(np.float32),
        "rope_s": np.stack([-s, s], axis=-1).reshape(T, HD).astype(np.float32),
    }


INPUTS = ["x", "c", "ctx", "c_ctx", "w_ada", "b_ada", "norm1_g", "w_in", "q_norm_g", "k_norm_g", "w_attn_o",
          "w_fourier", "w_out", "norm2_g", "w1", "w2", "final_norm_g"]


def kernel(**inputs):
    import concourse.bacc as bacc
    from concourse.bass_utils import run_bass_kernel_spmd

    nc = bacc.Bacc("TRN2", target_bir_lowering=False, num_devices=1, dynamic_dma_scratch_size=1024)
    arrays, args = {}, []
    for name in INPUTS:
        a = np.ascontiguousarray(inputs[name])
        if a.shape[0] == 1 and a.ndim > 1:
            a = a[0]
        arrays[f"in_{name}"] = a
    arrays |= {f"in_{name}": a for name, a in constants().items()}
    for name, a in arrays.items():
        args.append(nc.dram_tensor(name, a.shape, mybir.dt.from_np(a.dtype), kind="ExternalInput").ap())
    out = nc.dram_tensor("out_0", (T, D), F32, kind="ExternalOutput").ap()
    block_program(nc, *args, out)
    got = run_bass_kernel_spmd(nc, [arrays], core_ids=[0])
    return got.results[0]["out_0"].reshape(1, T, D)
```
